# Optimizing a Trainium2 kernel written in Bass

```python
import math
import jax, jax.numpy as jnp
from jax import lax
import numpy as np

D_MODEL = 1024
BATCH = 1
SEQ = 256
DEPTH = 1

M_HEADS = 4
M_HEAD_DIM = D_MODEL // (2 * M_HEADS)
M_CHUNK = 64
CONV_W = 4
A_HEADS = 8
A_KV_GROUPS = 2
A_HPG = A_HEADS // A_KV_GROUPS
A_HEAD_DIM = D_MODEL // (2 * A_HEADS)
CMP_BLOCK = 32
CMP_STRIDE = 16
SEL_BLOCK = 64
SEL_TOP_N = 16
WINDOW = 512
Q_BLOCK = 128
FORCED_BONUS = 1e3
NUM_BUCKETS = 32
MAX_DISTANCE = 128
N_EXPERTS = 32
TOP_K = 4
D_EXPERT = D_MODEL
SWIGLU_LIMIT = 7.0
SWIGLU_ALPHA = 1.702
EXPERT_ROWS = 128
EPS = 1e-6
D_MIX = M_HEADS * M_HEAD_DIM + A_HEADS * A_HEAD_DIM
SPLIT_SIZES = (
    M_HEADS * M_HEAD_DIM,
    M_HEADS * M_HEAD_DIM,
    M_HEADS * M_HEAD_DIM,
    M_HEADS * M_HEAD_DIM,
    M_HEADS,
    M_HEADS,
    A_HEADS * A_HEAD_DIM,
    A_KV_GROUPS * A_HEAD_DIM,
    A_KV_GROUPS * A_HEAD_DIM,
    A_KV_GROUPS * A_HEAD_DIM,
    A_KV_GROUPS * A_HEAD_DIM,
    A_KV_GROUPS * A_HEAD_DIM,
    A_KV_GROUPS * A_HEAD_DIM,
    A_HEADS * 3,
)
D_IN = sum(SPLIT_SIZES)


def rmsnorm(x, g):
    xf = x.astype(jnp.float32)
    y = xf * lax.rsqrt(jnp.mean(xf * xf, axis=-1, keepdims=True) + EPS)
    return (y * g.astype(jnp.float32)).astype(x.dtype)

def t5_bucket(dist):
    n = jnp.maximum(dist, 0)
    max_exact = NUM_BUCKETS // 2
    nf = jnp.maximum(n, 1).astype(jnp.float32)
    large = max_exact + (jnp.log(nf / max_exact) / math.log(MAX_DISTANCE / max_exact)
                         * (NUM_BUCKETS - max_exact)).astype(jnp.int32)
    large = jnp.minimum(large, NUM_BUCKETS - 1)
    return jnp.where(n < max_exact, n, large)

def masked_softmax(logits, valid):
    l = jnp.where(valid, logits, -jnp.inf)
    m = jnp.max(l, axis=-1, keepdims=True)
    m = jnp.where(jnp.isfinite(m), m, 0.0)
    e = jnp.where(valid, jnp.exp(l - m), 0.0)
    s = jnp.sum(e, axis=-1, keepdims=True)
    return e / jnp.where(s > 0, s, 1.0)

def causal_depthwise_conv(x, w):
    return lax.conv_general_dilated(
        x, w[:, None, :].astype(x.dtype), window_strides=(1,), padding=[(CONV_W - 1, 0)],
        dimension_numbers=('NWC', 'WIO', 'NWC'), feature_group_count=x.shape[-1])

def mlstm(q, k, v, i_pre, f_pre):
    dtype = q.dtype
    B_, S_, H_, Dh = q.shape
    nc = S_ // M_CHUNK
    f32 = jnp.float32

    def chunks(a):
        return a.astype(f32).reshape(B_, nc, M_CHUNK, H_, -1).transpose(0, 3, 1, 2, 4)

    qc = chunks(q)
    kc = chunks(k) * (Dh ** -0.5)
    vc = chunks(v)
    ig = i_pre.astype(f32).reshape(B_, nc, M_CHUNK, H_).transpose(0, 3, 1, 2)
    lf = jax.nn.log_sigmoid(f_pre.astype(f32)).reshape(B_, nc, M_CHUNK, H_).transpose(0, 3, 1, 2)
    g = jnp.cumsum(lf, axis=-1)
    G = g[..., -1]
    w_state = G[..., None] - g + ig

    def step(carry, xs):
        C, n, m = carry
        k_c, v_c, w_c, G_c = xs
        m_new = jnp.maximum(G_c + m, jnp.max(w_c, axis=-1))
        decay = jnp.exp(G_c + m - m_new)
        wexp = jnp.exp(w_c - m_new[..., None])
        C_new = decay[..., None, None] * C + jnp.einsum('bhl,bhld,bhle->bhde', wexp, k_c, v_c)
        n_new = decay[..., None] * n + jnp.einsum('bhl,bhld->bhd', wexp, k_c)
        return (C_new, n_new, m_new), (C, n, m)

    init = (jnp.zeros((B_, H_, Dh, Dh), f32), jnp.zeros((B_, H_, Dh), f32),
            jnp.full((B_, H_), -jnp.inf, f32))
    xs = (kc.transpose(2, 0, 1, 3, 4), vc.transpose(2, 0, 1, 3, 4),
          w_state.transpose(2, 0, 1, 3), G.transpose(2, 0, 1))
    _, (Cp, Np, Mp) = lax.scan(step, init, xs)
    Cp = Cp.transpose(1, 2, 0, 3, 4)
    Np = Np.transpose(1, 2, 0, 3)
    Mp = Mp.transpose(1, 2, 0)

    causal = jnp.tril(jnp.ones((M_CHUNK, M_CHUNK), bool))
    Dm = jnp.where(causal, g[..., :, None] - g[..., None, :] + ig[..., None, :], -jnp.inf)
    inter = g + Mp[..., None]
    m_tau = jnp.maximum(inter, jnp.max(Dm, axis=-1))
    Wm = jnp.exp(Dm - m_tau[..., None]) * jnp.einsum('bhcld,bhcsd->bhcls', qc, kc)
    inter_w = jnp.exp(inter - m_tau)
    num = (jnp.einsum('bhcls,bhcse->bhcle', Wm, vc)
           + inter_w[..., None] * jnp.einsum('bhcld,bhcde->bhcle', qc, Cp))
    den = jnp.sum(Wm, axis=-1) + inter_w * jnp.einsum('bhcld,bhcd->bhcl', qc, Np)
    h = num / jnp.maximum(jnp.abs(den), jnp.exp(-m_tau))[..., None]
    return h.transpose(0, 2, 3, 1, 4).reshape(B_, S_, H_ * Dh).astype(dtype)

def compress(k, pos_emb, w):
    S_ = k.shape[1]
    n_cmp = (S_ - CMP_BLOCK) // CMP_STRIDE + 1
    idx = jnp.arange(n_cmp)[:, None] * CMP_STRIDE + jnp.arange(CMP_BLOCK)[None, :]
    blocks = k[:, idx] + pos_emb[None, None, :, None, :]
    return jnp.einsum('bilgd,lde->bige', blocks, w)

def nsa(q, kc, vc, ks, vs, kw, vw, gates, rel_bias):
    B_, S_, G_, HPG_, Dh = q.shape
    scale = Dh ** -0.5
    f32 = jnp.float32
    n_cmp = kc.shape[1]
    n_sel = S_ // SEL_BLOCK
    top_n = min(SEL_TOP_N, n_sel)
    n_tok = top_n * SEL_BLOCK
    cmp_end = jnp.arange(n_cmp) * CMP_STRIDE + CMP_BLOCK - 1
    cmp_pos = jnp.arange(n_cmp)[:, None] * CMP_STRIDE + jnp.arange(CMP_BLOCK)[None, :]
    overlap = jnp.sum(jax.nn.one_hot(cmp_pos // SEL_BLOCK, n_sel, dtype=f32), axis=1) / CMP_BLOCK
    ks_blk = ks.reshape(B_, n_sel, SEL_BLOCK, G_, Dh).transpose(0, 3, 1, 2, 4).reshape(B_, G_, n_sel, SEL_BLOCK * Dh)
    vs_blk = vs.reshape(B_, n_sel, SEL_BLOCK, G_, Dh).transpose(0, 3, 1, 2, 4).reshape(B_, G_, n_sel, SEL_BLOCK * Dh)
    kw_pad = jnp.pad(kw, ((0, 0), (WINDOW, 0), (0, 0), (0, 0)))
    vw_pad = jnp.pad(vw, ((0, 0), (WINDOW, 0), (0, 0), (0, 0)))
    rb = rel_bias.reshape(NUM_BUCKETS, G_, HPG_)
    g_idx = jnp.arange(G_)[None, None, :, None]
    blk = jnp.arange(n_sel)
    sel_off = jnp.arange(SEL_BLOCK)
    win_off = jnp.arange(Q_BLOCK + WINDOW) - WINDOW

    def block(qb):
        q0 = qb * Q_BLOCK
        t = q0 + jnp.arange(Q_BLOCK)
        qq = lax.dynamic_slice_in_dim(q, q0, Q_BLOCK, axis=1)
        lc = jnp.einsum('bqghd,bigd->bqghi', qq, kc, preferred_element_type=f32) * scale
        lc = lc + rb[t5_bucket(t[:, None] - cmp_end[None, :])].transpose(0, 2, 3, 1)[None]
        valid_c = (cmp_end[None, :] <= t[:, None])[None, :, None, None, :]
        pc = masked_softmax(lc, valid_c)
        oc = jnp.einsum('bqghi,bigd->bqghd', pc, vc)
        ps = jnp.einsum('bqghi,ij->bqgj', pc, overlap)
        cur = t // SEL_BLOCK
        forced = (blk[None, :] == 0) | (blk[None, :] == cur[:, None]) | (blk[None, :] == cur[:, None] - 1)
        valid_b = blk[None, :] * SEL_BLOCK <= t[:, None]
        score = jnp.where(valid_b[None, :, None, :],
                          ps + jnp.where(forced, FORCED_BONUS, 0.0)[None, :, None, :], -jnp.inf)
        _, sel = lax.top_k(score, top_n)
        sel_t = sel.transpose(0, 2, 1, 3).reshape(B_, G_, Q_BLOCK * top_n)[..., None]
        kg = jnp.take_along_axis(ks_blk, sel_t, axis=2).reshape(B_, G_, Q_BLOCK, n_tok, Dh)
        vg = jnp.take_along_axis(vs_blk, sel_t, axis=2).reshape(B_, G_, Q_BLOCK, n_tok, Dh)
        tok = (sel[..., None] * SEL_BLOCK + sel_off).reshape(B_, Q_BLOCK, G_, n_tok)
        ls = jnp.einsum('bqghd,bgqnd->bqghn', qq, kg, preferred_element_type=f32) * scale
        bs = rb[t5_bucket(t[None, :, None, None] - tok), g_idx]
        ls = ls + bs.transpose(0, 1, 2, 4, 3)
        pss = masked_softmax(ls, (tok <= t[None, :, None, None])[:, :, :, None, :])
        osel = jnp.einsum('bqghn,bgqnd->bqghd', pss, vg)
        kwb = lax.dynamic_slice_in_dim(kw_pad, q0, Q_BLOCK + WINDOW, axis=1)
        vwb = lax.dynamic_slice_in_dim(vw_pad, q0, Q_BLOCK + WINDOW, axis=1)
        j = q0 + win_off
        dist = t[:, None] - j[None, :]
        valid_w = (j[None, :] >= 0) & (dist >= 0) & (dist < WINDOW)
        lw = jnp.einsum('bqghd,bkgd->bqghk', qq, kwb, preferred_element_type=f32) * scale
        lw = lw + rb[t5_bucket(dist)].transpose(0, 2, 3, 1)[None]
        pw = masked_softmax(lw, valid_w[None, :, None, None, :])
        ow = jnp.einsum('bqghk,bkgd->bqghd', pw, vwb)
        gg = lax.dynamic_slice_in_dim(gates, q0, Q_BLOCK, axis=1).astype(f32)
        o = gg[..., 0:1] * oc + gg[..., 1:2] * osel + gg[..., 2:3] * ow
        return o.reshape(B_, Q_BLOCK, G_ * HPG_ * Dh).astype(q.dtype)

    out = lax.map(block, jnp.arange(S_ // Q_BLOCK))
    return out.transpose(1, 0, 2, 3).reshape(B_, S_, G_ * HPG_ * Dh)

def moe(h, w_router, b_router, w_up, b_up, w_down, b_down):
    B_, S_, D_ = h.shape
    N = B_ * S_
    NK = N * TOP_K
    xf = h.reshape(N, D_)
    logits = jnp.dot(xf, w_router, preferred_element_type=jnp.float32) + b_router.astype(jnp.float32)
    vals, idx = lax.top_k(logits, TOP_K)
    gate = jax.nn.softmax(vals, axis=-1)
    e_flat = idx.reshape(NK)
    tok_flat = jnp.arange(NK) // TOP_K
    gate_flat = gate.reshape(NK)
    order = jnp.argsort(e_flat)
    sorted_e = e_flat[order]
    counts = jnp.bincount(e_flat, length=N_EXPERTS)
    starts = jnp.cumsum(counts) - counts
    padded = (counts + EXPERT_ROWS - 1) // EXPERT_ROWS * EXPERT_ROWS
    pends = jnp.cumsum(padded)
    pstarts = pends - padded
    dest = pstarts[sorted_e] + (jnp.arange(NK) - starts[sorted_e])
    R = NK + N_EXPERTS * EXPERT_ROWS
    n_blk = R // EXPERT_ROWS
    row_tok = jnp.full((R,), N, jnp.int32).at[dest].set(tok_flat[order])
    row_gate = jnp.zeros((R,), jnp.float32).at[dest].set(gate_flat[order])
    blk_e = jnp.minimum(jnp.sum(jnp.arange(n_blk)[:, None] * EXPERT_ROWS >= pends[None, :], axis=1),
                        N_EXPERTS - 1)
    x_pad = jnp.concatenate([xf, jnp.zeros((1, D_), xf.dtype)], axis=0)
    xin = x_pad[row_tok].reshape(n_blk, EXPERT_ROWS, D_)

    def expert_block(args):
        xb, eb = args
        up = jnp.dot(xb, w_up[eb]) + b_up[eb]
        glu, lin = jnp.split(up, 2, axis=-1)
        glu = jnp.minimum(glu, SWIGLU_LIMIT)
        lin = jnp.clip(lin, -SWIGLU_LIMIT, SWIGLU_LIMIT)
        act = glu * jax.nn.sigmoid(SWIGLU_ALPHA * glu) * (lin + 1.0)
        return jnp.dot(act, w_down[eb]) + b_down[eb]

    yb = lax.map(expert_block, (xin, blk_e)).reshape(R, D_)
    out = jnp.zeros((N + 1, D_), h.dtype).at[row_tok].add(yb * row_gate[:, None].astype(h.dtype))
    return out[:N].reshape(B_, S_, D_)

def first_inputs(seed: int = 0) -> dict:
    key = jax.random.key(seed)
    ks = jax.random.split(key, 24)
    nrm = lambda k, shape, s: jax.random.normal(k, shape, jnp.float32) * s
    L = DEPTH
    gate_base = jnp.concatenate([jnp.zeros((M_HEADS,), jnp.float32),
                                 jnp.linspace(3.0, 6.0, M_HEADS, dtype=jnp.float32)])
    return {
        "x": nrm(ks[0], (BATCH, SEQ, D_MODEL), 1.0),
        "c": nrm(ks[1], (BATCH, D_MODEL), 1.0),
        "w_ada": nrm(ks[2], (L, D_MODEL, 6 * D_MODEL), 0.5 * D_MODEL ** -0.5),
        "b_ada": nrm(ks[3], (L, 6 * D_MODEL), 0.02),
        "g_pre_mix": 1.0 + nrm(ks[4], (L, D_MODEL), 0.05),
        "g_post_mix": 1.0 + nrm(ks[5], (L, D_MODEL), 0.05),
        "g_pre_ffn": 1.0 + nrm(ks[6], (L, D_MODEL), 0.05),
        "g_post_ffn": 1.0 + nrm(ks[7], (L, D_MODEL), 0.05),
        "w_in": nrm(ks[8], (L, D_MODEL, D_IN), D_MODEL ** -0.5),
        "b_gates": gate_base + nrm(ks[9], (L, 2 * M_HEADS), 0.1),
        "conv_qk": nrm(ks[10], (L, CONV_W, 2 * M_HEADS * M_HEAD_DIM), CONV_W ** -0.5),
        "w_cmp_k": nrm(ks[11], (L, CMP_BLOCK, A_HEAD_DIM, A_HEAD_DIM), (CMP_BLOCK * A_HEAD_DIM) ** -0.5),
        "w_cmp_v": nrm(ks[12], (L, CMP_BLOCK, A_HEAD_DIM, A_HEAD_DIM), (CMP_BLOCK * A_HEAD_DIM) ** -0.5),
        "pos_cmp_k": nrm(ks[13], (L, CMP_BLOCK, A_HEAD_DIM), 0.1),
        "pos_cmp_v": nrm(ks[14], (L, CMP_BLOCK, A_HEAD_DIM), 0.1),
        "rel_bias": nrm(ks[15], (NUM_BUCKETS, A_HEADS), 0.5),
        "w_out": nrm(ks[16], (L, D_MIX, D_MODEL), D_MIX ** -0.5),
        "w_router": nrm(ks[17], (L, D_MODEL, N_EXPERTS), D_MODEL ** -0.5),
        "b_router": nrm(ks[18], (L, N_EXPERTS), 0.01),
        "w_up": nrm(ks[19], (L, N_EXPERTS, D_MODEL, 2 * D_EXPERT), D_MODEL ** -0.5),
        "b_up": nrm(ks[20], (L, N_EXPERTS, 2 * D_EXPERT), 0.01),
        "w_down": nrm(ks[21], (L, N_EXPERTS, D_EXPERT, D_MODEL), D_EXPERT ** -0.5),
        "b_down": nrm(ks[22], (L, N_EXPERTS, D_MODEL), 0.01),
    }

def first_block(x, c, w_ada, b_ada, g_pre_mix, g_post_mix, g_pre_ffn, g_post_ffn, w_in, b_gates,
              conv_qk, w_cmp_k, w_cmp_v, pos_cmp_k, pos_cmp_v, rel_bias, w_out, w_router, b_router,
              w_up, b_up, w_down, b_down):
    B_, S_, _ = x.shape
    split_at = np.cumsum(SPLIT_SIZES)[:-1].tolist()
    for l in range(DEPTH):
        mod = jnp.dot(jax.nn.silu(c), w_ada[l]) + b_ada[l]
        sh1, sc1, gt1, sh2, sc2, gt2 = [m[:, None, :] for m in jnp.split(mod, 6, axis=-1)]
        h = rmsnorm(x, g_pre_mix[l]) * (1.0 + sc1) + sh1
        z = jnp.dot(h, w_in[l])
        (q_m, k_m, v_m, o_m, i_m, f_m, q_a, kc_a, vc_a, ks_a, vs_a, kw_a, vw_a, g_a) = \
            jnp.split(z, split_at, axis=-1)
        qk = jax.nn.silu(causal_depthwise_conv(jnp.concatenate([q_m, k_m], axis=-1), conv_qk[l]))
        q_m, k_m = jnp.split(qk, 2, axis=-1)
        mh = lambda a: a.reshape(B_, S_, M_HEADS, M_HEAD_DIM)
        y_m = mlstm(mh(q_m), mh(k_m), mh(v_m),
                    i_m + b_gates[l, :M_HEADS], f_m + b_gates[l, M_HEADS:])
        y_m = y_m * jax.nn.sigmoid(o_m)
        kv = lambda a: a.reshape(B_, S_, A_KV_GROUPS, A_HEAD_DIM)
        kc = compress(kv(kc_a), pos_cmp_k[l], w_cmp_k[l])
        vc = compress(kv(vc_a), pos_cmp_v[l], w_cmp_v[l])
        y_a = nsa(q_a.reshape(B_, S_, A_KV_GROUPS, A_HPG, A_HEAD_DIM), kc, vc,
                  kv(ks_a), kv(vs_a), kv(kw_a), kv(vw_a),
                  jax.nn.sigmoid(g_a).reshape(B_, S_, A_KV_GROUPS, A_HPG, 3), rel_bias)
        y = jnp.dot(jnp.concatenate([y_m, y_a], axis=-1), w_out[l])
        x = x + gt1 * rmsnorm(y, g_post_mix[l])
        h2 = rmsnorm(x, g_pre_ffn[l]) * (1.0 + sc2) + sh2
        y2 = moe(h2, w_router[l], b_router[l], w_up[l], b_up[l], w_down[l], b_down[l])
        x = x + gt2 * rmsnorm(y2, g_post_ffn[l])
    return x


DEPTH_2 = 2

N_META = 16
D_ATTN = 512
D_REC = 512
D_MIX_2 = D_ATTN + D_REC
ATTN_HEADS = 4
ATTN_HEAD_DIM = 64
V_HEAD_DIM = 2 * ATTN_HEAD_DIM
ROPE_DIM = ATTN_HEAD_DIM // 4
ROPE_THETA = 500000.0
REC_BLOCKS = 8
REC_BLOCK_DIM = D_REC // REC_BLOCKS
CONV_WIDTH = 4
LRU_C = 8.0
D_FF = -(-8 * D_MODEL // (3 * 256)) * 256
N_IN = 3 * D_ATTN + 2 * D_REC


def rms_norm(x, g):
    xf = x.astype(jnp.float32)
    y = xf * lax.rsqrt(jnp.mean(xf * xf, axis=-1, keepdims=True) + EPS)
    return (y * g.astype(jnp.float32)).astype(x.dtype)

def rope_tables(T):
    inv = ROPE_THETA ** (-jnp.arange(0, ROPE_DIM, 2, dtype=jnp.float32) / ROPE_DIM)
    ang = jnp.arange(T, dtype=jnp.float32)[:, None] * inv[None, :]
    return jnp.cos(ang), jnp.sin(ang)

def apply_partial_rope(x, cos, sin):
    half = ROPE_DIM // 2
    c = cos[None, :, None, None, :].astype(x.dtype)
    s = sin[None, :, None, None, :].astype(x.dtype)
    x1 = x[..., :half]
    x2 = x[..., half:ROPE_DIM]
    return jnp.concatenate([x1 * c - x2 * s, x2 * c + x1 * s, x[..., ROPE_DIM:]], axis=-1)

def diff_attention(q, k, v, lam):
    B, T, H = q.shape[:3]
    nb = -(-T // Q_BLOCK)
    Tp = nb * Q_BLOCK
    padw = ((0, 0), (0, Tp - T), (0, 0), (0, 0), (0, 0))
    q = jnp.pad(q, padw)
    k = jnp.pad(k, padw)
    v = jnp.pad(v, padw[:4])
    qb = q.reshape(B, nb, Q_BLOCK, H, 2, ATTN_HEAD_DIM).transpose(1, 0, 2, 3, 4, 5)
    starts = jnp.arange(nb) * Q_BLOCK
    kpos = jnp.arange(Tp)
    scale = ATTN_HEAD_DIM ** -0.5

    def one_block(args):
        qblk, start = args
        s = jnp.einsum('bqhcd,bkhcd->bhcqk', qblk, k,
                       preferred_element_type=jnp.float32) * scale
        qpos = start + jnp.arange(Q_BLOCK)
        s = jnp.where(qpos[:, None] >= kpos[None, :], s, -jnp.inf)
        p = jax.nn.softmax(s, axis=-1)
        a = p[:, :, 0] - lam * p[:, :, 1]
        return jnp.einsum('bhqk,bkhe->bqhe', a.astype(v.dtype), v)

    o = lax.map(one_block, (qb, starts))
    return o.transpose(1, 0, 2, 3, 4).reshape(B, Tp, H, V_HEAD_DIM)[:, :T]

def rg_lru_branch(xr, gate, conv_w, conv_b, w_rg, b_rg, w_ig, b_ig, lru_L):
    B, T, _ = xr.shape
    xc = lax.conv_general_dilated(
        xr, conv_w[:, None, :].astype(xr.dtype), window_strides=(1,),
        padding=[(CONV_WIDTH - 1, 0)], dimension_numbers=('NWC', 'WIO', 'NWC'),
        feature_group_count=D_REC) + conv_b.astype(xr.dtype)
    xb = xc.reshape(B, T, REC_BLOCKS, REC_BLOCK_DIM)
    r = jax.nn.sigmoid((jnp.einsum('btnd,nde->btne', xb, w_rg).reshape(B, T, D_REC)
                        + b_rg).astype(jnp.float32))
    i = jax.nn.sigmoid((jnp.einsum('btnd,nde->btne', xb, w_ig).reshape(B, T, D_REC)
                        + b_ig).astype(jnp.float32))
    log_a = LRU_C * r * jax.nn.log_sigmoid(lru_L.astype(jnp.float32))
    a = jnp.exp(log_a)
    mult = jnp.sqrt(jnp.maximum(-jnp.expm1(2.0 * log_a), 0.0))
    mult = jnp.where(jnp.arange(T)[None, :, None] == 0, 1.0, mult)
    u = mult * i * xc.astype(jnp.float32)

    def combine(left, right):
        a1, b1 = left
        a2, b2 = right
        return a1 * a2, a2 * b1 + b2

    _, h = lax.associative_scan(combine, (a, u), axis=1)
    y = h * jax.nn.gelu(gate.astype(jnp.float32))
    return y.astype(xr.dtype)

def second_inputs(seed: int = 0) -> dict:
    key = jax.random.key(seed)
    ks = jax.random.split(key, 24)
    f32 = jnp.float32
    L = DEPTH_2

    def nrm(k, shape, scale):
        return jax.random.normal(k, shape, f32) * scale

    u = jax.random.uniform(ks[15], (L, D_REC), f32, 0.9, 0.999)
    s = u ** (1.0 / LRU_C)
    lru_L = jnp.log(s) - jnp.log1p(-s)
    return {
        "x": nrm(ks[0], (BATCH, SEQ, D_MODEL), 1.0),
        "meta_tokens": nrm(ks[1], (N_META, D_MODEL), 1.0),
        "norm_mix_g": 1.0 + nrm(ks[2], (L, D_MODEL), 0.02),
        "w_in": nrm(ks[3], (L, D_MODEL, N_IN), D_MODEL ** -0.5),
        "q_norm_g": 1.0 + nrm(ks[4], (L, ATTN_HEAD_DIM), 0.02),
        "k_norm_g": 1.0 + nrm(ks[5], (L, ATTN_HEAD_DIM), 0.02),
        "lambda_q1": nrm(ks[6], (L, ATTN_HEAD_DIM), 0.1),
        "lambda_k1": nrm(ks[7], (L, ATTN_HEAD_DIM), 0.1),
        "lambda_q2": nrm(ks[8], (L, ATTN_HEAD_DIM), 0.1),
        "lambda_k2": nrm(ks[9], (L, ATTN_HEAD_DIM), 0.1),
        "subln_g": 1.0 + nrm(ks[10], (L, V_HEAD_DIM), 0.02),
        "conv_w": nrm(ks[11], (L, CONV_WIDTH, D_REC), CONV_WIDTH ** -0.5),
        "conv_b": nrm(ks[12], (L, D_REC), 0.01),
        "w_rg": nrm(ks[13], (L, REC_BLOCKS, REC_BLOCK_DIM, REC_BLOCK_DIM), REC_BLOCK_DIM ** -0.5),
        "b_rg": nrm(ks[14], (L, D_REC), 0.01),
        "w_ig": nrm(ks[16], (L, REC_BLOCKS, REC_BLOCK_DIM, REC_BLOCK_DIM), REC_BLOCK_DIM ** -0.5),
        "b_ig": nrm(ks[17], (L, D_REC), 0.01),
        "lru_L": lru_L,
        "rec_norm_g": 1.0 + nrm(ks[18], (L, D_REC), 0.02),
        "w_out": nrm(ks[19], (L, D_MIX_2, D_MODEL), D_MIX_2 ** -0.5),
        "norm_ffn_g": 1.0 + nrm(ks[20], (L, D_MODEL), 0.02),
        "w_gu": nrm(ks[21], (L, D_MODEL, 2 * D_FF), D_MODEL ** -0.5),
        "w_down": nrm(ks[22], (L, D_FF, D_MODEL), D_FF ** -0.5),
    }

def second_block(x, meta_tokens, norm_mix_g, w_in, q_norm_g, k_norm_g, lambda_q1, lambda_k1,
              lambda_q2, lambda_k2, subln_g, conv_w, conv_b, w_rg, b_rg, w_ig, b_ig, lru_L,
              rec_norm_g, w_out, norm_ffn_g, w_gu, w_down):
    B = x.shape[0]
    meta = jnp.broadcast_to(meta_tokens.astype(x.dtype)[None], (B, N_META, D_MODEL))
    h = jnp.concatenate([meta, x], axis=1)
    T = h.shape[1]
    cos, sin = rope_tables(T)
    splits = [D_ATTN, 2 * D_ATTN, 3 * D_ATTN, 3 * D_ATTN + D_REC]

    for l in range(DEPTH_2):
        lam_init = 0.8 - 0.6 * math.exp(-0.3 * l)
        hn = rms_norm(h, norm_mix_g[l])
        proj = hn @ w_in[l]
        q, k, v, xr, gate = jnp.split(proj, splits, axis=-1)
        q = q.reshape(B, T, ATTN_HEADS, 2, ATTN_HEAD_DIM)
        k = k.reshape(B, T, ATTN_HEADS, 2, ATTN_HEAD_DIM)
        v = v.reshape(B, T, ATTN_HEADS, V_HEAD_DIM)
        q = apply_partial_rope(rms_norm(q, q_norm_g[l]), cos, sin)
        k = apply_partial_rope(rms_norm(k, k_norm_g[l]), cos, sin)
        lam = (jnp.exp(jnp.sum(lambda_q1[l].astype(jnp.float32) * lambda_k1[l].astype(jnp.float32)))
               - jnp.exp(jnp.sum(lambda_q2[l].astype(jnp.float32) * lambda_k2[l].astype(jnp.float32)))
               + lam_init)
        o_attn = diff_attention(q, k, v, lam)
        o_attn = (rms_norm(o_attn, subln_g[l]) * (1.0 - lam_init)).reshape(B, T, D_ATTN)
        o_rec = rg_lru_branch(xr, gate, conv_w[l], conv_b[l], w_rg[l], b_rg[l],
                              w_ig[l], b_ig[l], lru_L[l])
        o_rec = rms_norm(o_rec, rec_norm_g[l])
        h = h + jnp.concatenate([o_attn, o_rec], axis=-1) @ w_out[l]
        hn = rms_norm(h, norm_ffn_g[l])
        g, u = jnp.split(hn @ w_gu[l], [D_FF], axis=-1)
        h = h + (jax.nn.silu(g) * u) @ w_down[l]

    return h[:, N_META:, :]


def setup_inputs(seed=0):
    out = dict(first_inputs(seed))
    for name, value in second_inputs(seed + 1).items():
        if name != "x":
            out[name + "_2"] = value
    return out


def reference(
    x, c, w_ada, b_ada, g_pre_mix, g_post_mix, g_pre_ffn, g_post_ffn, w_in, b_gates, conv_qk,
    w_cmp_k, w_cmp_v, pos_cmp_k, pos_cmp_v, rel_bias, w_out, w_router, b_router, w_up, b_up,
    w_down, b_down, meta_tokens_2, norm_mix_g_2, w_in_2, q_norm_g_2, k_norm_g_2, lambda_q1_2,
    lambda_k1_2, lambda_q2_2, lambda_k2_2, subln_g_2, conv_w_2, conv_b_2, w_rg_2, b_rg_2,
    w_ig_2, b_ig_2, lru_L_2, rec_norm_g_2, w_out_2, norm_ffn_g_2, w_gu_2, w_down_2,
):
    x = first_block(
        x, c, w_ada, b_ada, g_pre_mix, g_post_mix, g_pre_ffn, g_post_ffn, w_in, b_gates,
        conv_qk, w_cmp_k, w_cmp_v, pos_cmp_k, pos_cmp_v, rel_bias, w_out, w_router, b_router,
        w_up, b_up, w_down, b_down,
    )
    return second_block(
        x, meta_tokens_2, norm_mix_g_2, w_in_2, q_norm_g_2, k_norm_g_2, lambda_q1_2,
        lambda_k1_2, lambda_q2_2, lambda_k2_2, subln_g_2, conv_w_2, conv_b_2, w_rg_2, b_rg_2,
        w_ig_2, b_ig_2, lru_L_2, rec_norm_g_2, w_out_2, norm_ffn_g_2, w_gu_2, w_down_2,
    )


_drawn_inputs = setup_inputs


def setup_inputs(seed=0):
    import zlib

    import numpy as np

    out = dict(_drawn_inputs(seed))
    spreads = {}
    factors = {'g_post_ffn': 3.16,
     'pos_cmp_k': 8.0,
     'b_router': 3.717,
     'b_up': 8.0,
     'b_down': 8.0,
     'q_norm_g_2': 8.0,
     'k_norm_g_2': 7.055,
     'lambda_q1_2': 3.279,
     'subln_g_2': 4.251,
     'b_rg_2': 8.0,
     'b_ig_2': 8.0,
     'rec_norm_g_2': 3.858,
     'norm_ffn_g_2': 3.72}
    for name, (base, spread) in spreads.items():
        noise = np.random.default_rng([zlib.crc32(name.encode()), seed]).standard_normal(out[name].shape)
        drawn = base * np.exp(spread * noise) if base else spread * noise
        out[name] = __import__('jax').numpy.asarray(drawn.astype(out[name].dtype))
    for name, factor in factors.items():
        out[name] = (out[name] * factor).astype(out[name].dtype)
    return out
```

```python
import math
from contextlib import ExitStack

import numpy as np

import concourse.bass as bass
from concourse import mybir

F32 = mybir.dt.float32
I32 = mybir.dt.int32
ALU = mybir.AluOpType
ACT = mybir.ActivationFunctionType
AX_X = mybir.AxisListType.X

P = 128
D = 1024
KD_ = D // P
S = 256
TT = S // P
META = 16
T2 = META + S
EPS = 1e-6
NEG = -1.0e30

MH, MD = 4, 128
AH, AG, AD = 8, 2, 64
CMP_BLOCK, CMP_STRIDE = 32, 16
NCMP = (S - CMP_BLOCK) // CMP_STRIDE + 1
BUCKETS, MAX_DIST = 32, 128
D_IN = 3360
C_I, C_F, C_QA, C_KC, C_KS, C_KW, C_GA = 2048, 2052, 2056, 2568, 2824, 3080, 3336
E = 32
TOPK = 4
CAP = 64
BLOCKS = S // CAP
OVER = (BLOCKS - 1) * E
ITEMS = S * TOPK // CAP
LIMIT, ALPHA = 7.0, 1.702

L2 = 2
H2, HD2 = 4, 64
ROPE = 16
REC = 512
FF = 2816
NF = FF // P
LRU_C = 8.0
LAM_INIT = [0.8 - 0.6 * math.exp(-0.3 * l) for l in range(L2)]

SLOTS, SLOT = 13, 2048
EARLY_SLOTS = 8
EXPERT_SLABS = 12
LAYER_SLABS = 52
VECTOR_STEPS = 48

CONST_COLS = dict(ident=128, flip=128, causal=128, before=128, pick=512, iota=2 * CAP, halves=128,
                  rot=128, future=128, future_tail=32, cos=T2, sin=T2, pair=2, number=1, column=96, rev=384, fwd=480)


def const_at():
    at, out = 0, {}
    for name, n in CONST_COLS.items():
        out[name] = (at, n)
        at += n
    return out, at


def buckets_of(dist):
    n = np.maximum(dist, 0)
    half = BUCKETS // 2
    nf = np.maximum(n, 1).astype(np.float32)
    large = half + (np.log(nf / np.float32(half)) / np.float32(math.log(MAX_DIST / half)) * np.float32(BUCKETS - half)).astype(np.int32)
    b = np.where(n < half, n, np.minimum(large, BUCKETS - 1))
    return np.where(dist < 0, BUCKETS, b)


def constants():
    at, width = const_at()
    c = np.zeros((P, width), np.float32)

    def put(name, v):
        a, n = at[name]
        c[:v.shape[0], a:a + v.shape[1]] = v

    i, j = np.arange(P)[:, None], np.arange(P)[None, :]
    put("ident", (i == j).astype(np.float32))
    put("flip", (i + j == P - 1).astype(np.float32))
    put("causal", (i <= j).astype(np.float32))
    put("before", (i < j).astype(np.float32))
    put("pick", np.repeat(np.eye(MH, dtype=np.float32), P, axis=1))
    put("iota", np.tile(np.arange(CAP, dtype=np.float32), (P, 2)))
    put("halves", (i // HD2 == j // HD2).astype(np.float32) / HD2)
    rot = np.zeros((P, P), np.float32)
    for b in (0, HD2):
        for m in range(ROPE // 2):
            rot[b + m + ROPE // 2, b + m] = -1.0
            rot[b + m, b + m + ROPE // 2] = 1.0
    put("rot", rot)
    put("future", np.where(j > i, NEG, 0.0).astype(np.float32))
    put("future_tail", np.where(np.arange(32)[None, :] > (i % 32), NEG, 0.0).astype(np.float32))
    inv = np.float32(500000.0) ** (-np.arange(0, ROPE, 2, dtype=np.float32) / np.float32(ROPE))
    ang = (np.arange(T2, dtype=np.float32)[:, None] * inv[None, :]).astype(np.float32)
    cos, sin = np.ones((P, T2), np.float32), np.zeros((P, T2), np.float32)
    for b in (0, HD2):
        for m in range(ROPE):
            cos[b + m] = np.cos(ang[:, m % (ROPE // 2)])
            sin[b + m] = np.sin(ang[:, m % (ROPE // 2)])
    put("cos", cos)
    put("sin", sin)
    put("pair", np.array([[1, 0], [0, 1], [-1, 0], [0, -1]], np.float32))
    put("number", np.arange(1, P + 1, dtype=np.float32)[:, None])
    put("column", np.tile(np.arange(E, E + OVER, dtype=np.float32), (P, 1)))
    one_hot = lambda b: (np.arange(BUCKETS + 1)[:, None] == b[None, :]).astype(np.float32)
    put("rev", one_hot(buckets_of(255 - np.arange(384))))
    put("fwd", one_hot(buckets_of(np.arange(480) - 255)))
    return c


ROWS1 = dict(b_ada=48, g_pre_mix=8, g_post_mix=8, g_pre_ffn=8, g_post_ffn=8, conv_qk=32, c=8)
ROWS2 = dict(norm_mix_g_2=16, norm_ffn_g_2=16, conv_w_2=32, conv_b_2=8, b_rg_2=8, b_ig_2=8, lru_L_2=8,
             rec_norm_g_2=8, subln_g_2=2, q_norm_g_2=2, k_norm_g_2=2)


def rows_at(rows, base):
    out, at = {}, 0
    for name, n in rows.items():
        out[name] = base + at
        at += n
    return out, at


def spread(ap, n):
    return ap.unsqueeze(1).broadcast_to([ap.shape[0], n, ap.shape[1]])


def spread_last(ap, n):
    return ap.unsqueeze(len(ap.shape)).broadcast_to(list(ap.shape) + [n])


class Steps:

    def __init__(self, eng, sem, base=0):
        self.eng, self.sem, self.base, self.n = eng, sem, base, 0

    def __call__(self, ins):
        self.n += 1
        ins.then_inc(self.sem, 1)
        self.eng.wait_ge(self.sem, self.base + self.n)


EARLY = ([("ada", j) for j in range(8)]
         + [("w_in", j) for j in range(13)]
         + [("ada", j) for j in range(8, 24)]
         + [("w_out", j) for j in range(4)])
EARLY_AT = {k: n for n, k in enumerate(EARLY)}
N_EARLY = len(EARLY)
W_IN_COLS = [0, 256, 512, 768, C_KC, C_QA, C_QA + 256, C_KS, C_KW, 1024, 1280, 1536, 1792]
MOE_STEPS = 6
USED_MAIN = N_EARLY + EXPERT_SLABS * E
USED_BLOCK2 = USED_MAIN + 1


def filled_before(slot):
    return sum(1 for n in range(N_EARLY) if n % EARLY_SLOTS == slot)


SEMS = """consts_in params_in x_in bias_rows_in small_in slab_used
params_turned params_ready x_turned residual_ready trel_made trel_out trel_copied bias_read
cmp_bias_made cmp_bias_ready bias_turned bias_ready
sq_ready norm_summed rstd_ready c_sig c_silu ada_made ada_rest_made mod_ready h_ready h2_ready
z_made z_out conv_ready conv_sig qk_ready kcv_ready cmp_made cmp_out const_ready
gate_abs gate_log rows_ready a_turned a_ready rows_spread decay_in decay_ready decay_masked
floor_ready qk_made w_ready num_made ym_ready
cmp_scored cmp_logit cmp_exp cmp_prob cmp_turned cmp_pt scored max_ready prob_ready prob_scaled
p_turned pt_ready pv_made ya_ready y_made y_out sq_y_ready y_summed x1_ready
var_ready y_var n2_var n2_sq n2_summed h2_turned h2_rows routed logits_ready logit_exp_in logit_exp gates_ready
placed listed list_turned table_ready biases_in gates_turned gates_t steps_v steps_a lam_in lam_exp lam_made lru_log""".split()

PASS_SEMS = """sel_ready hot_ready pg_ready bias_used u_free sig_ready act_ready gathered x_rows
scattered pg_turned pg_rows act_turned act_t y_rows acc_done steps""".split()

AGAIN = {
    "m_sq": ("params_turned", 1), "m_summed": ("params_ready", 1), "m_root": ("x_turned", 1), "m_y": ("trel_made", 1),
    "m_x": ("residual_ready", 1), "n_sq": ("trel_copied", 1), "n_summed": ("cmp_bias_made", 1),
    "n_root": ("cmp_bias_ready", 1), "n_h": ("bias_turned", 1), "z2_made": ("z_made", 15), "z2_out": ("z_out", 15),
    "qk_sq": ("bias_ready", 1), "qk_mean": ("sq_ready", 1), "qk_root": ("norm_summed", 1), "qk_normed": ("var_ready", 1),
    "qk_turned": ("rstd_ready", 1), "roped": ("c_sig", 1), "tail_scored": ("c_silu", 1), "tail_max": ("ada_made", 1),
    "tail_prob": ("ada_rest_made", 1), "tail_mixed": ("mod_ready", 1), "tail_turned": ("h_ready", 1),
    "tail_t": ("h2_ready", 1), "scored2": ("scored", 16), "max2": ("max_ready", 16), "prob2": ("prob_ready", 16),
    "mixed2": ("prob_scaled", 16), "turned2": ("p_turned", 16), "at2": ("pt_ready", 16), "o2_made": ("pv_made", 16),
    "o2_out": ("conv_ready", 4), "o2_mean": ("conv_sig", 4), "o2_root": ("qk_ready", 4), "attn_ready": ("kcv_ready", 1),
    "xc_ready": ("cmp_made", 1), "gates_made": ("cmp_out", 1), "gates_sig": ("gate_abs", 1), "lru_exp": ("rows_ready", 1),
    "mult_in": ("a_turned", 1), "mult_out": ("a_ready", 1), "gelu_in": ("gate_log", 1), "gelu_sig": ("rows_spread", 4),
    "rec_sq": ("decay_in", 4), "rec_mean": ("decay_ready", 4), "rec_root": ("decay_masked", 4), "mix_ready": ("floor_ready", 4),
    "out2_made": ("qk_made", 4), "out2_added": ("w_ready", 4), "f_sq": ("num_made", 4), "f_summed": ("ym_ready", 4),
    "f_root": ("cmp_scored", 1), "f_h": ("cmp_logit", 1), "gu_made": ("cmp_exp", 1), "g_sig": ("cmp_prob", 1),
    "gu_out": ("cmp_turned", 1), "down_made": ("cmp_pt", 1), "down_added": ("ya_ready", 4), "gate_w_in": None,
    "x_out": ("y_made", 4), "rows_out": ("y_out", 4), "stored": None, "steps2": ("steps_a", 1),
    "rot_out": ("sq_y_ready", 1),
}


def build(nc, x, c, w_ada, b_ada, g_pre_mix, g_post_mix, g_pre_ffn, g_post_ffn, w_in, b_gates, conv_qk,
          w_cmp_k, w_cmp_v, pos_cmp_k, pos_cmp_v, rel_bias, w_out, w_router, b_router, w_up, b_up,
          w_down, b_down, meta_tokens_2, norm_mix_g_2, w_in_2, q_norm_g_2, k_norm_g_2, lambda_q1_2,
          lambda_k1_2, lambda_q2_2, lambda_k2_2, subln_g_2, conv_w_2, conv_b_2, w_rg_2, b_rg_2,
          w_ig_2, b_ig_2, lru_L_2, rec_norm_g_2, w_out_2, norm_ffn_g_2, w_gu_2, w_down_2,
          consts, out):
    cat, cwidth = const_at()
    r1, n1 = rows_at(ROWS1, 0)
    r2, n2 = rows_at(ROWS2, n1)
    pos_at = n1 + n2
    n_cols = pos_at + 64
    trel = nc.dram_tensor("bias_by_distance", (AH, 384), F32)

    with ExitStack() as ctx:
        def sb(name, shape, dt=F32, stack=ctx):
            return stack.enter_context(nc.sbuf_tensor(name, shape, dt))

        s = {n: ctx.enter_context(nc.semaphore(n)) for n in SEMS}
        slot_in = [ctx.enter_context(nc.semaphore(f"slot_in{i}")) for i in range(SLOTS)]
        pb = [ctx.enter_context(nc.psum_tensor(f"bank{i}", [P, 512], F32)) for i in range(8)]

        ring = sb("ring", [P, SLOTS, SLOT])
        cst = sb("cst", [P, cwidth])
        C = {n: cst[:, a:a + w] for n, (a, w) in cat.items()}
        PC = sb("param_cols", [P, n_cols])
        xT = sb("xT", [P, KD_, T2])
        ones = sb("ones", [P, P])
        eps = sb("eps", [P, 1])
        mean_d = sb("mean_d", [P, P])
        hT = sb("hT", [P, KD_, T2])
        sq = sb("sq", [P, KD_, T2])
        yT = sb("yT", [P, KD_, T2])
        rstd = sb("rstd", [P, T2])
        mod = sb("modulation", [P, 48])
        gt1 = sb("gt1", [P, KD_])
        gt2 = sb("gt2", [P, KD_])
        A2 = sb("A2", [P, KD_])
        wr = sb("w_router_sb", [P, KD_, E])
        brr = sb("b_router_sb", [1, E])
        lam = sb("lam", [P, L2])
        LQ = sb("lambda_q", [4, HD2])
        LK = sb("lambda_k", [4, HD2])
        lam_sum = sb("lambda_sum", [4, 2])
        lru_c = sb("lru_decay", [P, 3, 8])
        gains = sb("gains", [P, 2, L2])
        xv = xT[:, :, META:T2]
        hv, sqv, yv = hT[:, :, 0:S], sq[:, :, 0:S], yT[:, :, 0:S]

        one = ExitStack()
        b1 = lambda name, shape, dt=F32: sb(name, shape, dt, one)
        PR1 = b1("param_rows1", [n1, P])
        PR2 = b1("param_rows2", [n2, P])
        POSR = b1("pos_rows", [64, P])
        xin = yT[:].rearrange("p k n -> p (k n)")[:, 0:TT * D].rearrange("p (t d) -> p t d", t=TT)
        rbx = b1("rel_bias_sb", [BUCKETS + 1, AH])
        BG = b1("gate_bias", [MH, 2])
        wg = b1("w_gate_rows", [P, KD_, 8])
        wga = b1("w_branch_gates", [P, KD_, 24])
        spare = ring[:, EARLY_SLOTS:SLOTS, :].rearrange("p a n -> p (a n)")
        spare_at = [0]

        def in_spare(n):
            a = spare_at[0]
            spare_at[0] += n
            assert spare_at[0] <= (SLOTS - EARLY_SLOTS) * SLOT
            return spare[:, a:a + n]

        WCK = in_spare(CMP_BLOCK * AD).rearrange("p (l e) -> p l e", l=CMP_BLOCK)
        WCV = in_spare(CMP_BLOCK * AD).rearrange("p (l e) -> p l e", l=CMP_BLOCK)
        ZC = in_spare(8 * (3 + S)).rearrange("p (k n) -> p k n", k=8)
        SG = in_spare(4 * S).rearrange("p (a k n) -> p a k n", a=2, k=2)
        KCV = in_spare(2 * S).rearrange("p (k n) -> p k n", k=2)
        KP = in_spare(4 * S).rearrange("p (k a n) -> p k a n", k=2, a=2)
        BQ = b1("bias_tiles", [P, AH, S])
        CB = b1("cmp_bias", [P, 2 * TT * 4 * NCMP])
        sc = b1("silu_c", [P, KD_])
        A1 = b1("A1", [P, KD_])
        GR = b1("gate_rows", [MH, 2, S])
        GW = b1("gate_work", [MH, 6, S])
        MM = b1("max_rows", [MH, 2, S])
        aC = b1("a_cols", [P, 2 * MH])
        GA = b1("branch_gates", [P, TT, 24])
        CV = b1("conv_out", [P, 8, S])
        GB = CV
        QT = b1("q_nsa", [P, 4, S])
        KD = b1("k_nsa", [P, 4, S])
        VS = b1("v_nsa", [P, 2, TT, P])
        VM = b1("v_mlstm", [P, TT, 512])
        metain = VM[0:META, :, :].rearrange("p t n -> p (t n)")
        SO = b1("sig_o", [P, 4, S])
        KC = b1("k_cmp", [P, 2, NCMP])
        VC = b1("v_cmp", [NCMP, 2, AD])
        idle_h = hT[:].rearrange("p k n -> p (k n)")
        idle_s = sq[:].rearrange("p k n -> p (k n)")
        two_of = lambda flat, a, n: flat[:, a:a + 2 * n].rearrange("p (b n) -> p b n", b=2)
        DE = b1("decay", [P, 2, 384])
        WT = two_of(idle_h, 0, 384)
        PT = two_of(idle_h, 768, 384)
        EN = two_of(idle_s, 0, S)
        DD = two_of(idle_s, 512, S)
        PR = two_of(idle_s, 1024, 384)
        CL = idle_s[:, 1792:1792 + 16 * NCMP].rearrange("p (a i) -> p a i", a=16)
        CM = idle_h[:, 1536:1600].rearrange("p (a i) -> p a i", a=4)
        TR = idle_h[0:AH, 0:384]
        PTC = CV[0:NCMP, :, :]
        NM = b1("neg_max", [P, 16, 2])
        SM = b1("prob_sum", [P, 16, 2])
        one.close()
        two = ExitStack()
        b2 = lambda name, shape, dt=F32: sb(name, shape, dt, two)
        E1 = 32 * BLOCKS + 1
        h2 = b2("h2_rows_sb", [P, TT, D])
        bup = b2("b_up_sb", [E, 2 * D])
        bdn = b2("b_down_sb", [E, D])
        LG = b2("logits", [P, TT, E])
        RW = b2("router_work", [P, 8, TT, E])
        RS = b2("router_stats", [P, 8, TT])
        V8 = b2("top8", [P, TT, 8])
        pmx = b2("place", [P, TT, E1])
        gx = b2("gate_of", [P, TT, E1])
        gtT = b2("gates_t_sb", [E, S])
        over = b2("over", [P, 6, OVER])
        pickc = b2("pick_col", [P, 1])
        lists = b2("list_rows", [1, 4, ITEMS + 1])
        table = b2("list_table", [1, 3, ITEMS + 1], I32)
        psel = b2("psel", [P, TT, CAP])
        pg = b2("pg", [P, TT, 2 * CAP])
        hot = b2("hot", [E, CAP])
        xe = b2("x_expert", [P, KD_, CAP])
        gl = b2("glu", [P, 512]); ln = b2("lin", [P, 512]); sg = b2("sig", [P, 512]); act_e = b2("act_e", [P, 512])
        actT = b2("act_t_e", [P, 4, P])
        ye = b2("y_expert", [P, 512])
        pgt = b2("pg_t", [P, S])
        two.close()

        def slab_src(kind, j):
            if kind == "ada":
                return w_ada[0, :, 256 * j:256 * j + 256].rearrange("(k p) n -> p k n", p=P)
            if kind == "w_in":
                return w_in[0, :, W_IN_COLS[j]:W_IN_COLS[j] + 256].rearrange("(k p) n -> p k n", p=P)
            return w_out[0, :, 256 * j:256 * j + 256].rearrange("(k p) n -> p k n", p=P)

        def slab(slot, k, n):
            return ring[:, slot, 0:k * n].rearrange("p (k n) -> p k n", k=k)

        def sync_block1(sp):
            sp.dma_start(cst[:], consts).then_inc(s["consts_in"], 16)
            sp.dma_start(xin[:], x[0].rearrange("(t p) d -> p t d", p=P)).then_inc(s["x_in"], 16)
            sp.dma_start(metain[:], meta_tokens_2).then_inc(s["x_in"], 16)
            for n, (kind, j) in enumerate(EARLY):
                if n >= EARLY_SLOTS:
                    sp.wait_ge(s["slab_used"], n - EARLY_SLOTS + 1)
                sp.dma_start(slab(n % EARLY_SLOTS, KD_, 256), slab_src(kind, j)).then_inc(slot_in[n % EARLY_SLOTS], 16)

        N_PARAM = 7 + 11 + 4
        N_SMALL = 3 + 4 + 2 + 4

        def scalar_loads(act):
            rows = dict(b_ada=b_ada[0].rearrange("(r p) -> r p", p=P), g_pre_mix=g_pre_mix[0].rearrange("(r p) -> r p", p=P),
                        g_post_mix=g_post_mix[0].rearrange("(r p) -> r p", p=P), g_pre_ffn=g_pre_ffn[0].rearrange("(r p) -> r p", p=P),
                        g_post_ffn=g_post_ffn[0].rearrange("(r p) -> r p", p=P),
                        conv_qk=conv_qk[0].rearrange("w (c p) -> (w c) p", p=P), c=c[0].rearrange("(r p) -> r p", p=P))
            for name, src in rows.items():
                a = r1[name]
                act.dma_start(PR1[a:a + ROWS1[name], :], src).then_inc(s["params_in"], 16)
            act.dma_start(rbx[0:BUCKETS, :], rel_bias).then_inc(s["bias_rows_in"], 16)
            flat = lambda v: v.rearrange("l (r p) -> (l r) p", p=P)
            rows = dict(norm_mix_g_2=flat(norm_mix_g_2), norm_ffn_g_2=flat(norm_ffn_g_2),
                        conv_w_2=conv_w_2.rearrange("l w (r p) -> (l w r) p", p=P), conv_b_2=flat(conv_b_2),
                        b_rg_2=flat(b_rg_2), b_ig_2=flat(b_ig_2), lru_L_2=flat(lru_L_2), rec_norm_g_2=flat(rec_norm_g_2),
                        subln_g_2=subln_g_2)
            for name, src in rows.items():
                a = r2[name] - n1
                act.dma_start(PR2[a:a + ROWS2[name], :], src).then_inc(s["params_in"], 16)
            for name, src in (("q_norm_g_2", q_norm_g_2), ("k_norm_g_2", k_norm_g_2)):
                a = r2[name] - n1
                act.dma_start(PR2[a:a + L2, :].rearrange("l (two d) -> l two d", two=2), spread(src, 2)).then_inc(s["params_in"], 16)
            for a, src in ((0, pos_cmp_k), (CMP_BLOCK, pos_cmp_v)):
                for half in (0, AD):
                    act.dma_start(POSR[a:a + CMP_BLOCK, half:half + AD], src[0]).then_inc(s["params_in"], 16)
            act.dma_start(BG[:], b_gates[0].rearrange("(a h) -> h a", a=2), allow_slow_non_contiguous=True).then_inc(s["small_in"], 16)
            act.dma_start(wg[:], w_in[0, :, C_I:C_I + 8].rearrange("(k p) n -> p k n", p=P)).then_inc(s["small_in"], 16)
            act.dma_start(wga[:], w_in[0, :, C_GA:C_GA + 24].rearrange("(k p) n -> p k n", p=P)).then_inc(s["small_in"], 16)
            for dst, src in ((WCK, w_cmp_k), (WCV, w_cmp_v)):
                for half in (0, AD):
                    act.dma_start(dst[half:half + AD, :, :], src[0].rearrange("l d e -> d l e")).then_inc(s["small_in"], 16)
            act.dma_start(wr[:], w_router[0].rearrange("(k p) n -> p k n", p=P)).then_inc(s["small_in"], 16)
            act.dma_start(brr[:], b_router).then_inc(s["small_in"], 16)
            for i, (dst, src) in enumerate(((LQ, lambda_q1_2), (LK, lambda_k1_2), (LQ, lambda_q2_2), (LK, lambda_k2_2))):
                act.dma_start(dst[2 * (i // 2):2 * (i // 2) + 2, :], src).then_inc(s["small_in"], 16)

        def gpsimd_block1(pool):
            pool.memset(rbx[BUCKETS:BUCKETS + 1, :], NEG).then_inc(s["const_ready"], 1)
            pool.wait_ge(s["const_ready"], 1)
            pool.memset(ones[:], 1.0).then_inc(s["const_ready"], 1)
            pool.memset(mean_d[:], 1.0 / D).then_inc(s["const_ready"], 1)
            pool.memset(ZC[:, :, 0:3], 0.0).then_inc(s["const_ready"], 1)
            pool.memset(eps[:], EPS).then_inc(s["const_ready"], 1)
            pool.wait_ge(s["const_ready"], 5)
            pool.wait_ge(s["consts_in"], 16)
            for h in range(MH):
                pool.wait_ge(s["decay_ready"], h + 1)
                d = DE[:, h % 2, :]
                blocks = DE[:, h % 2, 0:384].rearrange("p (b j) -> p b j", b=3)[:, 0:3:2, :]
                pool.tensor_tensor(blocks, blocks, spread(C["causal"], 2), ALU.mult).then_inc(s["decay_masked"], 1)

        def scalar_block1(act):
            st = Steps(act, s["steps_a"])
            def root(summed, bank, done):
                act.wait_ge(s[summed], 1)
                act.activation(rstd[:, 0:S], bank[:, 0:S], ACT.Sqrt, bias=eps[:]).then_inc(s[done], 1)

            act.wait_ge(s["x_turned"], 1)
            act.wait_ge(s["const_ready"], 5)
            for t in range(TT):
                for half in range(2):
                    act.activation(xT[:, 4 * half:4 * half + 4, META + P * t:META + P * t + P],
                                   pb[2 * t + half][:].rearrange("p (k n) -> p k n", k=4), ACT.Copy)
            act.activation(xT[:, :, 0:META], pb[5][:, 0:KD_ * META].rearrange("p (k n) -> p k n", k=KD_), ACT.Copy)\
               .then_inc(s["residual_ready"], 1)
            act.wait_ge(s["trel_made"], 1)
            act.activation(TR, pb[6][0:AH, 0:384], ACT.Copy).then_inc(s["trel_copied"], 1)
            act.wait_ge(s["trel_copied"], 1)
            act.dma_start(trel.ap(), TR).then_inc(s["trel_out"], 16)
            root("norm_summed", pb[5], "var_ready")
            act.wait_ge(s["trel_out"], 16)
            skewed = bass.AP(trel, 0, [[1, P], [384, AH], [1, S]])
            act.dma_start(GB[:], skewed).then_inc(s["bias_read"], 16)
            act.wait_ge(s["params_ready"], 1)
            act.activation(sc[:], PC[:, r1["c"]:r1["c"] + KD_], ACT.Sigmoid).then_inc(s["c_sig"], 1)
            act.wait_ge(s["bias_turned"], 1)
            for b in range(4):
                ins = act.activation(BQ[:, 2 * b:2 * b + 2, :], pb[b][:].rearrange("p (h n) -> p h n", h=2), ACT.Copy)
            ins.then_inc(s["bias_ready"], 1)

            def z_wait(u):
                act.wait_ge(s["z_made"], u + 1)

            def pair(u):
                return pb[u % 4][:].rearrange("p (k n) -> p k n", k=2)

            act.wait_ge(s["small_in"], 16 * N_SMALL)
            z_wait(0)
            act.activation(GR[:, 0, :], pb[0][0:MH, 0:S], ACT.Identity, bias=BG[:, 0:1])
            act.activation(GR[:, 1, :], pb[0][0:MH, S:2 * S], ACT.Identity, bias=BG[:, 1:2]).then_inc(s["z_out"], 1)
            z_wait(1)
            act.activation(GA[:], pb[1][:, 0:48].rearrange("p (t n) -> p t n", t=2), ACT.Sigmoid).then_inc(s["z_out"], 1)

            def conv_sigmoid(j):
                act.wait_ge(s["conv_ready"], j + 1)
                if j >= 2:
                    act.wait_ge(s["qk_ready"], j - 1)
                act.activation(SG[:, j % 2, :, :], CV[:, 2 * j:2 * j + 2, :], ACT.Sigmoid).then_inc(s["conv_sig"], 1)

            for j in range(4):
                z_wait(2 + j)
                if j == 0:
                    act.wait_ge(s["const_ready"], 4)
                act.activation(ZC[:, 2 * j:2 * j + 2, 3:3 + S], pair(2 + j), ACT.Copy).then_inc(s["z_out"], 1)
            z_wait(6)
            act.activation(KCV[:], pair(6), ACT.Copy).then_inc(s["z_out"], 1)
            conv_sigmoid(0)
            z_wait(7)
            act.activation(QT[:, 0:2, :], pair(7), ACT.Copy, scale=AD ** -0.5).then_inc(s["z_out"], 1)
            z_wait(8)
            act.activation(QT[:, 2:4, :], pair(8), ACT.Copy, scale=AD ** -0.5).then_inc(s["z_out"], 1)
            conv_sigmoid(1)
            for br in range(2):
                z_wait(9 + br)
                bank = pb[(9 + br) % 4]
                for g in range(AG):
                    for half in range(2):
                        act.activation(KD[AD * half:AD * half + AD, 2 * br + g, :], bank[AD * g:AD * g + AD, 0:S], ACT.Copy)
                act.activation(VS[:, br, :, :], bank[:, S:2 * S].rearrange("p (t n) -> p t n", t=2), ACT.Copy)\
                   .then_inc(s["z_out"], 1)
            conv_sigmoid(2)
            act.wait_ge(s["cmp_made"], 1)
            for g in range(AG):
                for half in range(2):
                    act.activation(KC[AD * half:AD * half + AD, g, :], pb[5 + g][0:AD, 0:NCMP], ACT.Copy)
                ins = act.activation(VC[:, g, :], pb[5 + g][0:NCMP, 32:32 + AD], ACT.Copy)
            ins.then_inc(s["cmp_out"], 1)
            for j in range(2):
                z_wait(11 + j)
                act.activation(VM[:, :, 256 * j:256 * j + 256], pair(11 + j), ACT.Copy).then_inc(s["z_out"], 1)
            conv_sigmoid(3)
            for j in range(2):
                z_wait(13 + j)
                act.activation(SO[:, 2 * j:2 * j + 2, :], pair(13 + j), ACT.Sigmoid).then_inc(s["z_out"], 1)

            act.wait_ge(s["gate_abs"], 1)
            st(act.activation(GW[:, 1, :], GW[:, 0, :], ACT.Exp))
            act.activation(GW[:, 2, :], GW[:, 1, :], ACT.Ln, bias=ones[0:MH, 0:1]).then_inc(s["gate_log"], 1)
            for h in range(MH):
                act.wait_ge(s["decay_in"], h + 1)
                act.activation(DE[:, h % 2, :], DE[:, h % 2, :], ACT.Exp, scale=-1.0).then_inc(s["decay_ready"], 1)
                act.activation(EN[:, h % 2, :], pb[h][:, S:2 * S], ACT.Exp, scale=-1.0).then_inc(s["floor_ready"], 1)

            act.wait_ge(s["cmp_logit"], 1)
            act.activation(CL[:], CL[:], ACT.Exp).then_inc(s["cmp_exp"], 1)
            act.wait_ge(s["cmp_turned"], 1)
            for b in range(4):
                ins = act.activation(PTC[:, 2 * b:2 * b + 2, :], pb[b][0:NCMP, :].rearrange("p (h n) -> p h n", h=2), ACT.Copy)
            ins.then_inc(s["cmp_pt"], 1)

            def unit_exp(u):
                act.wait_ge(s["max_ready"], u + 1)
                if u >= 2:
                    act.wait_ge(s["p_turned"], u - 1)
                bank = pb[u % 2]
                act.activation(PR[:, u % 2, 0:P], bank[:, 0:P], ACT.Exp, bias=NM[:, u, 0:1], accum_out=SM[:, u, 0:1])
                act.activation(PR[:, u % 2, P:384], bank[:, P:384], ACT.Exp, bias=NM[:, u, 1:2], accum_out=SM[:, u, 1:2])\
                   .then_inc(s["prob_ready"], 1)

            def unit_copy(u):
                act.wait_ge(s["p_turned"], u + 1)
                if u >= 2:
                    act.wait_ge(s["pv_made"], u - 1)
                act.activation(PT[:, u % 2, :], pb[2 + u % 2][:, 0:384], ACT.Copy).then_inc(s["pt_ready"], 1)
                if u % 4 == 3 and u > 3:
                    heads_out(u // 4 - 1)

            def heads_out(c):
                act.wait_ge(s["pv_made"], 4 * c + 4)
                act.activation(yv[:, 4 + c, :], pb[4 + c % 2][:, 0:S], ACT.Copy).then_inc(s["ya_ready"], 1)

            for u in range(17):
                if u < 16:
                    unit_exp(u)
                if u >= 1:
                    unit_copy(u - 1)
            heads_out(3)

            act.wait_ge(s["ym_ready"], 4)
            act.wait_ge(s["pv_made"], 16)
            act.dma_start(bup[:], b_up[0]).then_inc(s["biases_in"], 16)
            act.dma_start(bdn[:], b_down[0]).then_inc(s["biases_in"], 16)
            for j in range(4):
                act.wait_ge(s["y_made"], j + 1)
                act.activation(hv[:, 2 * j:2 * j + 2, :], pb[j][:].rearrange("p (k n) -> p k n", k=2), ACT.Copy).then_inc(s["y_out"], 1)
            root("y_summed", pb[4], "y_var")
            root("n2_summed", pb[5], "n2_var")
            for b in range(4):
                act.wait_ge(s["h2_turned"], b + 1)
                act.activation(h2[:, b // 2, 512 * (b % 2):512 * (b % 2) + 512], pb[b][:], ACT.Copy).then_inc(s["h2_rows"], 1)
            act.wait_ge(s["logit_exp_in"], 1)
            act.activation(RW[:, 4, :, :], RW[:, 3, :, :], ACT.Exp).then_inc(s["logit_exp"], 1)
            act.wait_ge(s["lam_in"], 1)
            act.activation(lam_sum[:, 1:2], lam_sum[:, 0:1], ACT.Exp).then_inc(s["lam_exp"], 1)
            st(act.activation(lru_c[:, 1, :], lru_c[:, 0, :], ACT.Exp))
            act.activation(lru_c[:, 2, :], lru_c[:, 1, :], ACT.Ln, bias=ones[:, 0:1]).then_inc(s["lru_log"], 1)
            act.wait_ge(s["gates_turned"], 1)
            act.activation(gtT[:], pb[5][0:E, 0:S], ACT.Copy).then_inc(s["gates_t"], 1)

        def vector_block1(dve):
            st = Steps(dve, s["steps_v"])
            tt, ts, stt = dve.tensor_tensor, dve.tensor_scalar, dve.scalar_tensor_tensor
            pc = lambda name, n: PC[:, r1[name]:r1[name] + n]
            dve.wait_ge(s["params_turned"], 1)
            dve.tensor_copy(PC[:], pb[4][:, 0:n_cols]).then_inc(s["params_ready"], 1)
            dve.wait_ge(s["residual_ready"], 1)
            tt(sqv, xv, xv, ALU.mult).then_inc(s["sq_ready"], 1)
            dve.wait_ge(s["cmp_bias_made"], 1)
            dve.tensor_copy(CB[:], pb[7][:, 0:240]).then_inc(s["cmp_bias_ready"], 1)
            dve.wait_ge(s["var_ready"], 1)
            dve.reciprocal(rstd[:, 0:S], rstd[:, 0:S]).then_inc(s["rstd_ready"], 1)
            dve.wait_ge(s["params_ready"], 1)
            dve.wait_ge(s["c_sig"], 1)
            tt(sc[:], sc[:], pc("c", KD_), ALU.mult).then_inc(s["c_silu"], 1)
            dve.wait_ge(s["rstd_ready"], 1)
            st(tt(sqv, xv, spread(rstd[:, 0:S], KD_), ALU.mult))
            dve.wait_ge(s["ada_made"], 1)
            st(tt(mod[:, 0:16], pb[6][:, 0:16], PC[:, 0:16], ALU.add))
            st(stt(A1[:], mod[:, 8:16], 1.0, pc("g_pre_mix", KD_), ALU.add, ALU.mult))
            for k in range(KD_):
                ins = ts(hv[:, k, :], sqv[:, k, :], A1[:, k:k + 1], mod[:, k:k + 1], ALU.mult, ALU.add)
            ins.then_inc(s["h_ready"], 1)

            def conv(j):
                dve.wait_ge(s["z_out"], 3 + j)
                cw = lambda w, ch: PC[:, r1["conv_qk"] + 8 * w + ch:r1["conv_qk"] + 8 * w + ch + 1]
                for w in (3, 2, 1, 0):
                    for ch in (2 * j, 2 * j + 1):
                        src = ZC[:, ch, w:w + S]
                        if w == 3:
                            ins = ts(CV[:, ch, :], src, cw(w, ch), None, ALU.mult)
                        else:
                            ins = stt(CV[:, ch, :], src, cw(w, ch), CV[:, ch, :], ALU.mult, ALU.add)
                    if w:
                        st(ins)
                ins.then_inc(s["conv_ready"], 1)

            def silu(j):
                dve.wait_ge(s["conv_sig"], j + 1)
                dve.wait_ge(s["conv_ready"], j + 1)
                tt(CV[:, 2 * j:2 * j + 2, :], CV[:, 2 * j:2 * j + 2, :], SG[:, j % 2, :, :], ALU.mult).then_inc(s["qk_ready"], 1)

            conv(0)
            conv(1)
            dve.wait_ge(s["z_out"], 7)
            for kv in range(2):
                for half in range(2):
                    a = pos_at + CMP_BLOCK * kv + CMP_STRIDE * half
                    ins = tt(KP[:, kv, half, :].rearrange("p (j r) -> p j r", r=CMP_STRIDE),
                             KCV[:, kv, :].rearrange("p (j r) -> p j r", r=CMP_STRIDE),
                             spread(PC[:, a:a + CMP_STRIDE], S // CMP_STRIDE), ALU.add)
            ins.then_inc(s["kcv_ready"], 1)
            silu(0)
            conv(2)
            silu(1)
            conv(3)
            silu(2)
            f, ig = GR[:, 1, :], GR[:, 0, :]
            st(stt(GW[:, 0, :], f, -1.0, f, ALU.mult, ALU.min))
            dve.sem_inc(s["gate_abs"], 1)
            silu(3)
            dve.wait_ge(s["gate_log"], 1)
            st(stt(GW[:, 3, :], f, 0.0, GW[:, 2, :], ALU.min, ALU.subtract))
            row1 = ones[0:MH, 0:1].broadcast_to([MH, S])
            st(dve.tensor_tensor_scan(GW[:, 4, :], row1, GW[:, 3, :], 0.0, ALU.mult, ALU.add))
            st(tt(GW[:, 5, :], ig, GW[:, 4, :], ALU.subtract))
            st(dve.tensor_tensor_scan(MM[:, 0, :], row1, GW[:, 5, :], -3.0e38, ALU.mult, ALU.max))
            tt(MM[:, 1, :], MM[:, 0, :], GW[:, 4, :], ALU.add).then_inc(s["rows_ready"], 1)
            dve.wait_ge(s["a_turned"], 1)
            dve.tensor_copy(aC[:], pb[4][:, 0:2 * MH]).then_inc(s["a_ready"], 1)
            dve.wait_ge(s["a_ready"], 1)
            dve.wait_ge(s["ada_rest_made"], 1)
            st(tt(mod[:, 16:48], pb[7][:, 0:32], PC[:, 16:48], ALU.add))
            tt(gt1[:], mod[:, 16:24], pc("g_post_mix", KD_), ALU.mult)
            tt(gt2[:], mod[:, 40:48], pc("g_post_ffn", KD_), ALU.mult)
            stt(A2[:], mod[:, 32:40], 1.0, pc("g_pre_ffn", KD_), ALU.add, ALU.mult).then_inc(s["mod_ready"], 1)

            def decay(h):
                dve.wait_ge(s["rows_spread"], h + 1)
                if h >= 2:
                    dve.wait_ge(s["w_ready"], h - 1)
                ts(DE[:, h % 2, 0:S], pb[h][:, 0:S], aC[:, h:h + 1], 0.0, ALU.subtract, ALU.max)
                ts(DE[:, h % 2, S:384], pb[h][:, P:S], aC[:, MH + h:MH + h + 1], 0.0, ALU.subtract, ALU.max)\
                    .then_inc(s["decay_in"], 1)

            def weights(h):
                dve.wait_ge(s["qk_made"], h + 1)
                dve.wait_ge(s["decay_masked"], h + 1)
                if h >= 2:
                    dve.wait_ge(s["num_made"], h - 1)
                stt(WT[:, h % 2, :], pb[4 + h % 2][:, 0:384], MD ** -0.5, DE[:, h % 2, :], ALU.mult, ALU.mult)\
                    .then_inc(s["w_ready"], 1)

            def head_out(h):
                dve.wait_ge(s["num_made"], h + 1)
                dve.wait_ge(s["floor_ready"], h + 1)
                bank = pb[6 + h % 2]
                dd = DD[:, h % 2, :]
                st(stt(dd, bank[:, S:2 * S], -1.0, EN[:, h % 2, :], ALU.mult, ALU.max))
                st(tt(dd, bank[:, S:2 * S], dd, ALU.max))
                st(dve.reciprocal(dd, dd))
                st(tt(dd, dd, SO[:, h, :], ALU.mult))
                tt(yv[:, h, :], bank[:, 0:S], dd, ALU.mult).then_inc(s["ym_ready"], 1)

            decay(0)
            decay(1)
            weights(0)
            for h in range(MH):
                if h + 1 < MH:
                    weights(h + 1)
                head_out(h)
                if h + 2 < MH:
                    decay(h + 2)

            dve.wait_ge(s["cmp_scored"], 1)
            for par in range(2):
                ins = tt(CL[:, 8 * par:8 * par + 8, :], pb[par][:, 0:120].rearrange("p (a i) -> p a i", i=NCMP),
                         CB[:, 120 * par:120 * par + 120].rearrange("p (a i) -> p a i", i=NCMP), ALU.add)
            st(ins)
            st(dve.tensor_reduce(CM[:, 0, :], CL[:], AX_X, ALU.max))
            st(ts(CM[:, 0, :], CM[:, 0, :], -1.0e29, None, ALU.max))
            tt(CL[:], CL[:], spread_last(CM[:, 0, :], NCMP), ALU.subtract).then_inc(s["cmp_logit"], 1)
            dve.wait_ge(s["cmp_exp"], 1)
            st(dve.tensor_reduce(CM[:, 1, :], CL[:], AX_X, ALU.add))
            st(ts(CM[:, 1, :], CM[:, 1, :], 1.0e-30, None, ALU.max))
            st(dve.reciprocal(CM[:, 2, :], CM[:, 1, :]))
            for par in range(2):
                gate = GA[:].rearrange("p q (hh par b) -> p par q hh b", par=2, b=3)[:, par, :, :, 0]
                ins = tt(CM[:, 3, 8 * par:8 * par + 8].rearrange("p (q hh) -> p q hh", q=2),
                         CM[:, 2, 8 * par:8 * par + 8].rearrange("p (q hh) -> p q hh", q=2), gate, ALU.mult)
            st(ins)
            tt(CL[:], CL[:], spread_last(CM[:, 3, :], NCMP), ALU.mult).then_inc(s["cmp_prob"], 1)

            def unit_max(u):
                dve.wait_ge(s["scored"], u + 1)
                dve.tensor_reduce(NM[:, u, 0:1], pb[u % 2][:, 0:P], AX_X, ALU.max, negate=True)
                dve.tensor_reduce(NM[:, u, 1:2], pb[u % 2][:, P:384], AX_X, ALU.max, negate=True).then_inc(s["max_ready"], 1)

            def unit_scale(u):
                h, br = u // 2, u % 2
                dve.wait_ge(s["prob_ready"], u + 1)
                st(dve.reciprocal(SM[:, u, :], SM[:, u, :]))
                g = 3 * h + 1 + br
                st(tt(SM[:, u, :], SM[:, u, :], GA[:, :, g], ALU.mult))
                ts(PR[:, u % 2, 0:P], PR[:, u % 2, 0:P], SM[:, u, 0:1], None, ALU.mult)
                ts(PR[:, u % 2, P:384], PR[:, u % 2, P:384], SM[:, u, 1:2], None, ALU.mult).then_inc(s["prob_scaled"], 1)

            unit_max(0)
            for u in range(16):
                if u + 1 < 16:
                    unit_max(u + 1)
                unit_scale(u)

            dve.wait_ge(s["y_out"], 4)
            tt(sqv, hv, hv, ALU.mult).then_inc(s["sq_y_ready"], 1)
            dve.wait_ge(s["y_var"], 1)
            st(dve.reciprocal(rstd[:, 0:S], rstd[:, 0:S]))
            st(tt(sqv, hv, spread(rstd[:, 0:S], KD_), ALU.mult))
            for k in range(KD_):
                ins = stt(xv[:, k, :], sqv[:, k, :], gt1[:, k:k + 1], xv[:, k, :], ALU.mult, ALU.add)
            ins.then_inc(s["x1_ready"], 1)
            dve.wait_ge(s["x1_ready"], 1)
            tt(sqv, xv, xv, ALU.mult).then_inc(s["n2_sq"], 1)
            dve.wait_ge(s["n2_var"], 1)
            st(dve.reciprocal(rstd[:, 0:S], rstd[:, 0:S]))
            st(tt(sqv, xv, spread(rstd[:, 0:S], KD_), ALU.mult))
            for k in range(KD_):
                ins = ts(hv[:, k, :], sqv[:, k, :], A2[:, k:k + 1], mod[:, 24 + k:25 + k], ALU.mult, ALU.add)
            ins.then_inc(s["h2_ready"], 1)

            dve.wait_ge(s["routed"], 1)
            st(dve.tensor_copy(LG[:], pb[6][:, 0:2 * E].rearrange("p (t e) -> p t e", t=TT)))
            for t in range(TT):
                ins = dve.max(V8[:, t, :], LG[:, t, :])
            st(ins)
            v4 = spread_last(V8[:, :, TOPK - 1], E)
            tt(RW[:, 3, :, :], LG[:], spread_last(V8[:, :, 0], E), ALU.subtract).then_inc(s["logit_exp_in"], 1)
            tt(RW[:, 0, :, :], LG[:], v4, ALU.is_gt)
            st(tt(RW[:, 1, :, :], LG[:], v4, ALU.is_equal))
            dve.tensor_reduce(RS[:, 0, :], RW[:, 0, :, :], AX_X, ALU.add)
            for t in range(TT):
                ins = dve.tensor_tensor_scan(RW[:, 2, t, :], ones[:, 0:E], RW[:, 1, t, :], 0.0, ALU.mult, ALU.add)
            st(ins)
            st(ts(RS[:, 0, :], RS[:, 0, :], -1.0, float(TOPK), ALU.mult, ALU.add))
            st(tt(RW[:, 2, :, :], RW[:, 2, :, :], spread_last(RS[:, 0, :], E), ALU.is_le))
            st(tt(RW[:, 2, :, :], RW[:, 2, :, :], RW[:, 1, :, :], ALU.mult))
            picked = RW[:, 5, :, :]
            st(tt(picked, RW[:, 2, :, :], RW[:, 0, :, :], ALU.add))
            dve.sem_inc(s["logits_ready"], 1)
            dve.wait_ge(s["logit_exp"], 1)
            st(tt(RW[:, 4, :, :], RW[:, 4, :, :], picked, ALU.mult))
            st(dve.tensor_reduce(RS[:, 1, :], RW[:, 4, :, :], AX_X, ALU.add))
            st(dve.reciprocal(RS[:, 2, :], RS[:, 1, :]))
            st(tt(gx[:, :, 0:E], RW[:, 4, :, :], spread_last(RS[:, 2, :], E), ALU.mult))
            for b in range(1, BLOCKS):
                dve.tensor_copy(gx[:, :, E * b:E * b + E], gx[:, :, 0:E])
            dve.memset(gx[:, :, E1 - 1:E1], 0.0)
            dve.memset(pmx[:, :, E1 - 1:E1], -1.0).then_inc(s["gates_ready"], 1)
            lru = PC[:, r2["lru_L_2"]:r2["lru_L_2"] + 8]
            st(tt(LQ[:], LQ[:], LK[:], ALU.mult))
            dve.tensor_reduce(lam_sum[:, 0:1], LQ[:], AX_X, ALU.add)
            stt(lru_c[:, 0, :], lru, -1.0, lru, ALU.mult, ALU.min).then_inc(s["lam_in"], 1)
            ts(gains[:, 0, :], PC[:, r2["q_norm_g_2"]:r2["q_norm_g_2"] + L2], HD2 ** -0.5, None, ALU.mult)
            for l in range(L2):
                a = r2["subln_g_2"] + l
                ts(gains[:, 1, l:l + 1], PC[:, a:a + 1], 1.0 - LAM_INIT[l], None, ALU.mult)
            dve.wait_ge(s["placed"], 1)
            places = pb[7][:, 0:2 * E].rearrange("p (t e) -> p t e", t=TT)
            st(stt(pmx[:, :, 0:E], places, 1.0, picked, ALU.add, ALU.mult))
            st(ts(pmx[:, :, 0:E], pmx[:, :, 0:E], -1.0, None, ALU.add))
            for b in range(1, BLOCKS):
                ins = ts(pmx[:, :, E * b:E * b + E], pmx[:, :, 0:E], -float(CAP * b), None, ALU.add)
            dve.wait_ge(s["lru_log"], 1)
            st(stt(lru_c[:, 0, :], lru, 0.0, lru_c[:, 2, :], ALU.min, ALU.subtract))
            ts(lru_c[:, 1, :], lru_c[:, 0, :], LRU_C, None, ALU.mult)
            ts(lru_c[:, 2, :], lru_c[:, 0, :], -LRU_C, None, ALU.mult)
            dve.wait_ge(s["lam_made"], 1)
            for l in range(L2):
                ts(lam[:, l:l + 1], pb[4][:, l:l + 1], -1.0, -LAM_INIT[l], ALU.mult, ALU.add)
            st(dve.tensor_copy(over[:, 5, 0:E], pb[7][:, 2 * E:3 * E]))
            for b in range(1, BLOCKS):
                ins = ts(over[:, 0, E * (b - 1):E * b], over[:, 5, 0:E], float(CAP * b), None, ALU.is_gt)
            st(ins)
            st(dve.tensor_tensor_scan(over[:, 1, :], ones[:, 0:OVER], over[:, 0, :], 0.0, ALU.mult, ALU.add))
            st(stt(over[:, 2, :], over[:, 1, :], C["number"][:, 0:1], over[:, 0, :], ALU.is_equal, ALU.mult))
            st(tt(over[:, 3, :], over[:, 2, :], C["column"][:, 0:OVER], ALU.mult))
            dve.tensor_reduce(pickc[:], over[:, 3, :], AX_X, ALU.add).then_inc(s["listed"], 1)
            dve.wait_ge(s["list_turned"], 1)
            items = lists[0:1, 0, :]
            st(dve.tensor_copy(items, pb[6][0:1, 256:256 + ITEMS + 1]))
            st(ts(lists[0:1, 1, :], items, 64.0, -32.0, ALU.is_ge, ALU.mult))
            st(ts(lists[0:1, 2, :], items, 96.0, -32.0, ALU.is_ge, ALU.mult))
            st(tt(lists[0:1, 1, :], lists[0:1, 1, :], lists[0:1, 2, :], ALU.add))
            st(stt(lists[0:1, 3, :], items, -32.0, lists[0:1, 1, :], ALU.add, ALU.add))
            st(ts(lists[0:1, 3, :], lists[0:1, 3, :], 0.0, None, ALU.max))
            dve.tensor_copy(table[0:1, 0, :], items)
            dve.tensor_copy(table[0:1, 1, :], lists[0:1, 3, :])
            dve.tensor_copy(table[0:1, 2, :], over[0:1, 1, OVER - 1:OVER].broadcast_to([1, ITEMS + 1])).then_inc(s["table_ready"], 1)

        def tensor_block1(pe):
            mm, tp = pe.matmul, pe.transpose
            pe.wait_ge(s["consts_in"], 16)
            pe.wait_ge(s["params_in"], 16 * N_PARAM)
            ident = C["ident"]
            tp(pb[4][:, 0:n1], PR1[:], ident[0:n1, 0:n1])
            tp(pb[4][:, n1:pos_at], PR2[:], ident[0:n2, 0:n2])
            tp(pb[4][:, pos_at:n_cols], POSR[:], ident[0:64, 0:64]).then_inc(s["params_turned"], 1)
            pe.wait_ge(s["x_in"], 32)
            for t in range(TT):
                for k in range(KD_):
                    tp(pb[2 * t + k // 4][:, P * (k % 4):P * (k % 4) + P], xin[:, t, P * k:P * k + P], ident)
            for k in range(KD_):
                ins = tp(pb[5][:, META * k:META * k + META], metain[:, P * k:P * k + P], ident[0:META, 0:META])
            ins.then_inc(s["x_turned"], 1)
            pe.wait_ge(s["bias_rows_in"], 16)
            pe.wait_ge(s["const_ready"], 3)
            nb = BUCKETS + 1
            mm(pb[6][0:AH, 0:384], rbx[:], C["rev"][0:nb, :], start=True, stop=True).then_inc(s["trel_made"], 1)
            by_par = rbx[:].rearrange("b (hh par) -> b par hh", par=2)
            for t in range(TT):
                for i in range(NCMP):
                    a = P * t - CMP_STRIDE * i + 224
                    dst = pb[7][:, 0:240].rearrange("p (par q hh i) -> p par q hh i", par=2, q=2, hh=4)[:, :, t, :, i]
                    ins = mm(dst, C["fwd"][0:nb, a:a + P], by_par, start=True, stop=True)
            ins.then_inc(s["cmp_bias_made"], 1)
            pe.wait_ge(s["sq_ready"], 1)
            for k in range(KD_):
                ins = mm(pb[5][:, 0:S], mean_d[:], sqv[:, k, :], start=(k == 0), stop=(k == KD_ - 1))
            ins.then_inc(s["norm_summed"], 1)
            pe.wait_ge(s["bias_read"], 16)
            for h in range(AH):
                ins = mm(pb[h // 2][:, S * (h % 2):S * (h % 2) + S], C["flip"], GB[:, h, :], start=True, stop=True)
            ins.then_inc(s["bias_turned"], 1)

            def arrive(n):
                pe.wait_ge(slot_in[n % EARLY_SLOTS], 16 * (n // EARLY_SLOTS + 1))
                return slab(n % EARLY_SLOTS, KD_, 256)

            def modulation(j, dst):
                w = arrive(EARLY_AT["ada", j])
                for m in range(2):
                    for k in range(KD_):
                        ins = mm(dst[:, m:m + 1], w[:, k, P * m:P * m + P], sc[:, k:k + 1], start=(k == 0), stop=(k == KD_ - 1))
                ins.then_inc(s["slab_used"], 1)

            pe.wait_ge(s["c_silu"], 1)
            pe.wait_ge(s["trel_copied"], 1)
            for j in range(8):
                modulation(j, pb[6][:, 2 * j:2 * j + 2])
            mm(pb[6][:, 32:33], mean_d[:], ones[:, 0:1], start=True, stop=True).then_inc(s["ada_made"], 1)

            def unit(u):
                if u >= 4:
                    pe.wait_ge(s["z_out"], u - 3)
                return pb[u % 4]

            def columns(dst, w, n):
                for k in range(KD_):
                    ins = mm(dst, w(k), hv[:, k, :], start=(k == 0), stop=(k == KD_ - 1))
                return ins

            def rows(dst, w, t):
                for k in range(KD_):
                    ins = mm(dst, hv[:, k, P * t:P * t + P], w(k), start=(k == 0), stop=(k == KD_ - 1))
                return ins

            pe.wait_ge(s["bias_ready"], 1)
            pe.wait_ge(s["small_in"], 16 * N_SMALL)
            pe.wait_ge(s["h_ready"], 1)
            columns(unit(0)[0:MH, 0:S], lambda k: wg[:, k, 0:4], 4)
            columns(pb[0][0:MH, S:2 * S], lambda k: wg[:, k, 4:8], 4).then_inc(s["z_made"], 1)
            for t in range(TT):
                ins = rows(unit(1)[:, 24 * t:24 * t + 24], lambda k: wga[:, k, :], t)
            ins.then_inc(s["z_made"], 1)

            def column_unit(u, j, scale=None):
                w = arrive(EARLY_AT["w_in", j])
                bank = unit(u)
                for m in range(2):
                    ins = columns(bank[:, S * m:S * m + S], lambda k: w[:, k, P * m:P * m + P], P)
                ins.then_inc(s["z_made"], 1)

            def used():
                mm(pb[6][:, 32:33], mean_d[:], ones[:, 0:1], start=True, stop=True).then_inc(s["slab_used"], 1)

            for j in range(7):
                column_unit(2 + j, j)
                used()
            for br in range(2):
                w = arrive(EARLY_AT["w_in", 7 + br])
                bank = unit(9 + br)
                columns(bank[:, 0:S], lambda k: w[:, k, 0:P], P)
                for t in range(TT):
                    ins = rows(bank[:, S + P * t:S + P * t + P], lambda k: w[:, k, P:2 * P], t)
                ins.then_inc(s["z_made"], 1)
                used()
            pe.wait_ge(s["kcv_ready"], 1)
            pe.wait_ge(s["rstd_ready"], 1)
            pe.wait_ge(s["rstd_ready"], 1)
            for kv in range(2):
                for g in range(AG):
                    for l in range(CMP_BLOCK):
                        half, r = l // CMP_STRIDE, l % CMP_STRIDE
                        data = KP[AD * g:AD * g + AD, kv, half, :].rearrange("p (j r) -> p j r", r=CMP_STRIDE)[:, half:half + NCMP, r]
                        if kv == 0:
                            ins = mm(pb[5 + g][0:AD, 0:NCMP], WCK[AD * g:AD * g + AD, l, :], data, start=(l == 0), stop=(l == 31))
                        else:
                            ins = mm(pb[5 + g][0:NCMP, 32:32 + AD], data, WCV[AD * g:AD * g + AD, l, :], start=(l == 0), stop=(l == 31))
            ins.then_inc(s["cmp_made"], 1)
            for j in range(2):
                w = arrive(EARLY_AT["w_in", 9 + j])
                bank = unit(11 + j)
                for t in range(TT):
                    ins = rows(bank[:, S * t:S * t + S], lambda k: w[:, k, :], t)
                ins.then_inc(s["z_made"], 1)
                mm(pb[4][:, 300:301], mean_d[:], ones[:, 0:1], start=True, stop=True).then_inc(s["slab_used"], 1)
            for j in range(2):
                column_unit(13 + j, 11 + j)
                mm(pb[4][:, 300:301], mean_d[:], ones[:, 0:1], start=True, stop=True).then_inc(s["slab_used"], 1)
            pe.wait_ge(s["cmp_bias_ready"], 1)
            for j in range(8, 24):
                modulation(j, pb[7][:, 2 * (j - 8):2 * (j - 8) + 2])
            mm(pb[7][:, 64:65], mean_d[:], ones[:, 0:1], start=True, stop=True).then_inc(s["ada_rest_made"], 1)

            pe.wait_ge(s["rows_ready"], 1)
            pe.wait_ge(s["params_ready"], 1)
            for t in range(TT):
                ins = tp(pb[4][:, MH * t:MH * t + MH], GW[:, 5, P * t:P * t + P], ident[0:MH, 0:MH])
            ins.then_inc(s["a_turned"], 1)
            pe.wait_ge(s["z_out"], 15)
            for h in range(MH):
                mm(pb[h][:], C["pick"][0:MH, P * h:P * h + P], MM[:].rearrange("h a n -> h (a n)"), start=True, stop=True)\
                    .then_inc(s["rows_spread"], 1)

            pe.wait_ge(s["qk_ready"], 4)
            pe.wait_ge(s["a_ready"], 1)

            def qk(h):
                if h >= 2:
                    pe.wait_ge(s["w_ready"], h - 1)
                bank = pb[4 + h % 2]
                mm(bank[:, 0:S], CV[:, 4 + h, 0:P], CV[:, h, :], start=True, stop=True)
                mm(bank[:, S:384], CV[:, 4 + h, P:S], CV[:, h, P:S], start=True, stop=True).then_inc(s["qk_made"], 1)

            def numden(h):
                pe.wait_ge(s["w_ready"], h + 1)
                if h >= 2:
                    pe.wait_ge(s["ym_ready"], h - 1)
                bank, w = pb[6 + h % 2], WT[:, h % 2, :]
                mm(bank[:, 0:S], VM[:, 0, P * h:P * h + P], w[:, 0:S], start=True, stop=False)
                mm(bank[:, P:S], VM[:, 1, P * h:P * h + P], w[:, S:384], start=False, stop=True)
                mm(bank[:, S:2 * S], ones[:], w[:, 0:S], start=True, stop=False)
                mm(bank[:, S + P:2 * S], ones[:], w[:, S:384], start=False, stop=True).then_inc(s["num_made"], 1)

            pe.wait_ge(s["cmp_out"], 1)
            pe.wait_ge(s["mod_ready"], 1)
            qk(0)
            for h in range(MH):
                if h + 1 < MH:
                    qk(h + 1)
                numden(h)

            pe.wait_ge(s["floor_ready"], 4)
            pe.wait_ge(s["decay_in"], 4)
            half = lambda h: slice(AD * (h % 2), AD * (h % 2) + AD)
            for h in range(AH):
                for t in range(TT):
                    a = NCMP * (4 * t + h // 2)
                    ins = mm(pb[h % 2][:, a:a + NCMP], QT[half(h), h // 2, P * t:P * t + P], KC[half(h), h // 4, :], start=True, stop=True)
            ins.then_inc(s["cmp_scored"], 1)
            pe.wait_ge(s["cmp_prob"], 1)
            for h in range(AH):
                for t in range(TT):
                    ins = tp(pb[h // 2][0:NCMP, S * (h % 2) + P * t:S * (h % 2) + P * t + P], CL[:, 8 * (h % 2) + 4 * t + h // 2, :], ident)
            ins.then_inc(s["cmp_turned"], 1)

            def scores(u):
                h, br = u // 2, u % 2
                if u >= 2:
                    pe.wait_ge(s["prob_ready"], u - 1)
                bank, key = pb[u % 2], KD[half(h), 2 * br + h // 4, :]
                mm(bank[:, 0:P], ident, BQ[:, h, P:S], start=True, stop=False)
                mm(bank[:, 0:P], QT[half(h), h // 2, 0:P], key[:, 0:P], start=False, stop=True)
                mm(bank[:, P:384], ident, BQ[:, h, :], start=True, stop=False)
                mm(bank[:, P:384], QT[half(h), h // 2, P:S], key, start=False, stop=True).then_inc(s["scored"], 1)

            def turn(u):
                pe.wait_ge(s["prob_scaled"], u + 1)
                if u >= 2:
                    pe.wait_ge(s["pt_ready"], u - 1)
                for b in range(3):
                    ins = tp(pb[2 + u % 2][:, P * b:P * b + P], PR[:, u % 2, P * b:P * b + P], ident)
                ins.then_inc(s["p_turned"], 1)

            def values(u):
                h, br = u // 2, u % 2
                c, g = h // 2, h // 4
                if u % 4 == 0 and c >= 2:
                    pe.wait_ge(s["ya_ready"], c - 1)
                pe.wait_ge(s["pt_ready"], u + 1)
                dst, p, v = pb[4 + c % 2][half(h), :], PT[:, u % 2, :], slice(AD * g, AD * g + AD)
                mm(dst[:, 0:S], VS[:, br, 0, v], p[:, 0:S], start=(br == 0), stop=False)
                ins = mm(dst[:, P:S], VS[:, br, 1, v], p[:, S:384], start=False, stop=False)
                if br:
                    ins = mm(dst[:, 0:S], VC[:, g, :], PTC[:, h, :], start=False, stop=True)
                ins.then_inc(s["pv_made"], 1)

            pe.wait_ge(s["cmp_pt"], 1)
            pe.wait_ge(s["ym_ready"], 4)
            scores(0)
            for u in range(16):
                if u + 1 < 16:
                    scores(u + 1)
                turn(u)
                if u >= 1:
                    values(u - 1)
            values(15)

            pe.wait_ge(s["ya_ready"], 4)
            for j in range(4):
                w = arrive(EARLY_AT["w_out", j])
                for m in range(2):
                    for k in range(KD_):
                        ins = mm(pb[j][:, S * m:S * m + S], w[:, k, P * m:P * m + P], yv[:, k, :], start=(k == 0), stop=(k == KD_ - 1))
                ins.then_inc(s["y_made"], 1)
                mm(pb[6][:, 32:33], mean_d[:], ones[:, 0:1], start=True, stop=True).then_inc(s["slab_used"], 1)
            pe.wait_ge(s["sq_y_ready"], 1)
            for k in range(KD_):
                ins = mm(pb[4][:, 0:S], mean_d[:], sqv[:, k, :], start=(k == 0), stop=(k == KD_ - 1))
            ins.then_inc(s["y_summed"], 1)
            pe.wait_ge(s["n2_sq"], 1)
            for k in range(KD_):
                ins = mm(pb[5][:, 0:S], mean_d[:], sqv[:, k, :], start=(k == 0), stop=(k == KD_ - 1))
            ins.then_inc(s["n2_summed"], 1)
            pe.wait_ge(s["h2_ready"], 1)
            for t in range(TT):
                for k in range(KD_):
                    mm(pb[6][:, E * t:E * t + E], hv[:, k, P * t:P * t + P], wr[:, k, :], start=(k == 0), stop=False)
                ins = mm(pb[6][:, E * t:E * t + E], ones[0:1, :], brr[:], start=False, stop=True)
            ins.then_inc(s["routed"], 1)
            for b in range(4):
                for i in range(4):
                    k = 4 * (b % 2) + i
                    ins = tp(pb[b][:, P * i:P * i + P], hv[:, k, P * (b // 2):P * (b // 2) + P], ident)
                ins.then_inc(s["h2_turned"], 1)
            pe.wait_ge(s["logits_ready"], 1)
            m0, m1 = RW[:, 5, 0, :], RW[:, 5, 1, :]
            mm(pb[7][:, 0:E], C["before"], m0, start=True, stop=True)
            mm(pb[7][:, E:2 * E], ones[:], m0, start=True, stop=False)
            mm(pb[7][:, E:2 * E], C["before"], m1, start=False, stop=True)
            mm(pb[7][:, 2 * E:3 * E], ones[:], m0, start=True, stop=False)
            mm(pb[7][:, 2 * E:3 * E], ones[:], m1, start=False, stop=True).then_inc(s["placed"], 1)
            pe.wait_ge(s["lam_exp"], 1)
            mm(pb[4][:, 0:2], lam_sum[:, 1:2].broadcast_to([4, P]), C["pair"][0:4, :], start=True, stop=True).then_inc(s["lam_made"], 1)
            pe.wait_ge(s["listed"], 1)
            tp(pb[6][0:1, 256:256 + ITEMS + 1], pickc[0:ITEMS + 1, :], ident[0:ITEMS + 1, 0:ITEMS + 1]).then_inc(s["list_turned"], 1)
            for t in range(TT):
                ins = tp(pb[5][0:E, P * t:P * t + P], gx[:, t, 0:E], ident)
            ins.then_inc(s["gates_turned"], 1)

        q1 = {n: ctx.enter_context(nc.semaphore(f"main_{n}")) for n in PASS_SEMS}
        q2 = {n: ctx.enter_context(nc.semaphore(f"extra_{n}")) for n in PASS_SEMS}
        extra_in = ctx.enter_context(nc.semaphore("extra_slabs_in"))
        used1, used2 = (s["slab_used"], N_EARLY), (ctx.enter_context(nc.semaphore("extra_slab_used")), EXPERT_SLABS)
        bankU0, bankU1, bankY, bankG = pb[0], pb[1], pb[2], pb[3]
        FIRST = [1, 2, 3, 4, 8, 9, 10, 11, 5, 6, 7, 0]

        def expert_slab(e, j):
            if j < 8:
                return ring[:, j, :], w_up[0, e, P * j:P * j + P, :]
            r = 2 * P * (j - 8)
            return slab(j, 2, D), w_down[0, e, r:r + 2 * P, :].rearrange("(a p) n -> p a n", p=P)

        def sync_experts(sp):
            for j in FIRST:
                if j < EARLY_SLOTS:
                    sp.wait_ge(s["slab_used"], max(n for n in range(N_EARLY) if n % EARLY_SLOTS == j) + 1)
                elif j == EARLY_SLOTS:
                    sp.wait_ge(s["qk_ready"], 4)
                    sp.wait_ge(s["cmp_out"], 1)
                dst, src = expert_slab(0, j)
                sp.dma_start(dst, src).then_inc(slot_in[j], 16)
            with sp.Fori(1, E) as e:
                for j in range(EXPERT_SLABS):
                    sp.wait_ge(s["slab_used"], N_EARLY + EXPERT_SLABS * (e - 1) + j + 1)
                    dst, src = expert_slab(e, j)
                    sp.dma_start(dst, src).then_inc(slot_in[j], 16)
            sp.wait_ge(s["table_ready"], 1)
            n = sp.value_load(table[0:1, 2, 0:1], min_val=0, max_val=ITEMS)
            with sp.If(n > 0):
                sp.wait_ge(s["slab_used"], USED_BLOCK2)
                sp.sem_inc(used2[0], EXPERT_SLABS)
                with sp.Fori(0, n) as m:
                    e = sp.value_load(table[0:1, 1, bass.ds(m, 1)], min_val=0, max_val=E - 1)
                    for j in range(EXPERT_SLABS):
                        sp.wait_ge(used2[0], EXPERT_SLABS * m + j + 1)
                        dst, src = expert_slab(e, j)
                        sp.dma_start(dst, src).then_inc(extra_in, 16)
                sp.wait_ge(q2["acc_done"], 1)

        def tensor_pass(pe, q, used, count, arrived):
            mm, tp, ident = pe.matmul, pe.transpose, C["ident"]
            used_sem, used_base = used

            def gather(i):
                pe.wait_ge(q["sel_ready"], i + 1)
                for k in range(KD_):
                    for t in range(TT):
                        ins = mm(bankG[:, CAP * k:CAP * k + CAP], h2[:, t, P * k:P * k + P], psel[:, t, :], start=(t == 0), stop=(t == 1))
                ins.then_inc(q["gathered"], 1)

            def scatter(i, done):
                pe.wait_ge(q["y_rows"], i + 1)
                pe.wait_ge(q["pg_rows"], i + 1)
                for k in range(4):
                    for half in range(2):
                        bank = pb[4 + 2 * half + k // 2]
                        r = slice(CAP * half, CAP * half + CAP)
                        ins = mm(bank[:, S * (k % 2):S * (k % 2) + S], ye[r, P * k:P * k + P], pgt[r, :],
                                 start=False, stop=False, skip_group_check=True)
                ins.then_inc(done, 1)

            gather(0)
            with pe.Fori(0, count) as i:
                pe.wait_ge(q["hot_ready"], i + 1)
                pe.wait_ge(q["u_free"], i + 1)
                for b, bank in enumerate((bankU0, bankU1)):
                    for half in range(2):
                        a = D * b + 512 * half
                        ins = mm(bank[CAP * half:CAP * half + CAP, :], hot[:], bup[:, a:a + 512], start=True, stop=False)
                ins.then_inc(q["bias_used"], 1)
                pe.wait_ge(q["x_rows"], i + 1)
                for k in range(KD_):
                    pe.wait_ge(*arrived(k, i))
                    for b, bank in enumerate((bankU0, bankU1)):
                        for half in range(2):
                            a = D * b + 512 * half
                            ins = mm(bank[CAP * half:CAP * half + CAP, :], xe[:, k, :], ring[:, k, a:a + 512], start=False, stop=(k == KD_ - 1))
                    ins.then_inc(used_sem, 1)
                pe.wait_ge(q["pg_rows"], i + 1)
                gather(i + 1)
                scatter(i, q["scattered"])
                pe.wait_ge(q["pg_ready"], i + 1)
                pe.wait_ge(q["x_rows"], i + 2)
                for t in range(TT):
                    ins = tp(bankG[:, P * t:P * t + P], pg[:, t, :], ident)
                ins.then_inc(q["pg_turned"], 1)
                pe.wait_ge(q["act_ready"], i + 1)
                for c in range(4):
                    ins = tp(bankY[:, P * c:P * c + P], act_e[:, P * c:P * c + P], ident)
                ins.then_inc(q["act_turned"], 1)
                pe.wait_ge(q["act_t"], i + 1)
                for k in range(KD_):
                    if k % 2 == 0:
                        pe.wait_ge(*arrived(8 + k // 2, i))
                    w = slab(8 + k // 2, 2, D)[:, k % 2, :]
                    rows_ = actT[:, k % 4, CAP * (k // 4):CAP * (k // 4) + CAP]
                    for half in range(2):
                        ins = mm(bankY[CAP * half:CAP * half + CAP, :], rows_, w[:, 512 * half:512 * half + 512], start=(k == 0), stop=(k == KD_ - 1))
                    if k % 2:
                        ins.then_inc(used_sem, 1)
            scatter(count, q["acc_done"])

        def tensor_experts(pe):
            pe.wait_ge(s["gates_t"], 1)
            pe.wait_ge(s["table_ready"], 1)
            pe.wait_ge(s["biases_in"], 32)
            pe.wait_ge(s["h2_rows"], 4)
            for k in range(KD_):
                pe.matmul(pb[4 + k // 2][:, S * (k % 2):S * (k % 2) + S], bdn[:, P * k:P * k + P], gtT[:],
                          start=(k % 2 == 0), stop=False, skip_group_check=True)
            tensor_pass(pe, q1, used1, E, lambda j, i: (slot_in[j], 16 * (filled_before(j) + i + 1)))
            pe.matmul(bankG[:, 0:1], mean_d[:], ones[:, 0:1], start=True, stop=True).then_inc(s["slab_used"], 1)
            n = pe.value_load(table[0:1, 2, 0:1], min_val=0, max_val=ITEMS)
            with pe.If(n > 0):
                tensor_pass(pe, q2, used2, n, lambda j, i: (extra_in, 16 * EXPERT_SLABS * (i + 1)))

        def scalar_pass(act, q, used, count):
            used_sem, used_base = used
            act.wait_ge(q["gathered"], 1)
            act.activation(xe[:], bankG[:].rearrange("p (k n) -> p k n", k=KD_), ACT.Copy).then_inc(q["x_rows"], 1)
            with act.Fori(0, count) as i:
                act.wait_ge(q["u_free"], i + 2)
                act.activation(sg[:], gl[:], ACT.Sigmoid, scale=ALPHA).then_inc(q["sig_ready"], 1)
                act.wait_ge(q["gathered"], i + 2)
                act.activation(xe[:], bankG[:].rearrange("p (k n) -> p k n", k=KD_), ACT.Copy).then_inc(q["x_rows"], 1)
                act.wait_ge(q["pg_turned"], i + 2)
                act.wait_ge(q["scattered"], i + 1)
                act.activation(pgt[:], bankG[:, 0:S], ACT.Copy).then_inc(q["pg_rows"], 1)
                act.wait_ge(used_sem, used_base + EXPERT_SLABS * i + EXPERT_SLABS)
                act.activation(ye[:], bankY[:], ACT.Copy).then_inc(q["y_rows"], 1)
            act.wait_ge(q["acc_done"], 1)

        def scalar_experts(act):
            scalar_pass(act, q1, used1, E)
            n = act.value_load(table[0:1, 2, 0:1], min_val=0, max_val=ITEMS)
            with act.If(n > 0):
                scalar_pass(act, q2, used2, n)

        def vector_pass(dve, q, used, count, place, expert):
            ts = dve.tensor_scalar
            used_sem, used_base = used

            def select(j):
                for t in range(TT):
                    ins = ts(psel[:, t, :], C["iota"][:, 0:CAP], pmx[:, t, bass.ds(j, 1)], None, ALU.is_equal)
                ins.then_inc(q["sel_ready"], 1)

            def one_hot(e):
                dve.tensor_copy(hot[:], cst[0:E, bass.ds(cat["ident"][0] + e, 1)].broadcast_to([E, CAP])).then_inc(q["hot_ready"], 1)

            dve.memset(ye[:], 0.0).then_inc(q["y_rows"], 1)
            dve.memset(pgt[:], 0.0).then_inc(q["pg_rows"], 1)
            dve.sem_inc(q["u_free"], 1)
            dve.sem_inc(q["pg_turned"], 1)
            select(place(0))
            one_hot(expert(0))
            with dve.Fori(0, count) as i:
                dve.wait_ge(q["gathered"], i + 1)
                select(place(i + 1))
                dve.wait_ge(q["bias_used"], i + 1)
                one_hot(expert(i + 1))
                dve.wait_ge(q["pg_turned"], i + 1)
                j = place(i)
                for t in range(TT):
                    ins = ts(pg[:, t, :], C["iota"], pmx[:, t, bass.ds(j, 1)], gx[:, t, bass.ds(j, 1)], ALU.is_equal, ALU.mult)
                ins.then_inc(q["pg_ready"], 1)
                dve.wait_ge(used_sem, used_base + EXPERT_SLABS * i + 8)
                ts(gl[:], bankU0[:], LIMIT, None, ALU.min)
                ts(ln[:], bankU1[:], LIMIT, -LIMIT, ALU.min, ALU.max).then_inc(q["u_free"], 1)
                dve.wait_ge(q["u_free"], i + 2)
                dve.scalar_tensor_tensor(ln[:], ln[:], 1.0, gl[:], ALU.add, ALU.mult).then_inc(q["steps"], 1)
                dve.wait_ge(q["steps"], i + 1)
                dve.wait_ge(q["sig_ready"], i + 1)
                dve.tensor_tensor(act_e[:], ln[:], sg[:], ALU.mult).then_inc(q["act_ready"], 1)
                dve.wait_ge(q["act_turned"], i + 1)
                dve.tensor_copy(actT[:], bankY[:].rearrange("p (c n) -> p c n", c=4)).then_inc(q["act_t"], 1)
            dve.wait_ge(q["acc_done"], 1)

        def vector_experts(dve):
            dve.wait_ge(s["table_ready"], 1)
            dve.wait_ge(s["gates_ready"], 1)
            vector_pass(dve, q1, used1, E, lambda i: i, lambda i: i)
            n = dve.value_load(table[0:1, 2, 0:1], min_val=0, max_val=ITEMS)
            with dve.If(n > 0):
                vector_pass(dve, q2, used2, n,
                            lambda i: dve.value_load(table[0:1, 0, bass.ds(i, 1)], min_val=0, max_val=E1 - 1),
                            lambda i: dve.value_load(table[0:1, 1, bass.ds(i, 1)], min_val=0, max_val=E - 1))

        three = ExitStack()
        b3 = lambda name, shape, dt=F32: sb(name, shape, dt, three)
        QK = b3("qk2", [P, 8, T2])
        V2 = b3("v2", [P, 3, 512])
        PB = b3("probs2", [P, 2, 2, 384])
        PL = b3("probs_tail", [P, 2, T2])
        AT = b3("attn_t", [P, 2, 384])
        ST = b3("attn_stats", [P, 2, 2, 4])
        WG = b3("w_gates2", [P, 2, 4, HD2])
        FA = b3("ffn_act", [P, NF, T2])
        ST2 = b3("attn_stats2", [P, 2, 2, 4])
        three.close()
        FS = PB[:].rearrange("p a c n -> p (a c n)")[:, 0:4 * T2].rearrange("p (k n) -> p k n", k=4)
        FSv = FS
        flat_fa = FA[:].rearrange("p k n -> p (k n)")
        XR = flat_fa[:, 0:4 * (T2 + 3)].rearrange("p (k n) -> p k n", k=4)
        part = lambda i: flat_fa[:, 1100 + 4 * T2 * i:1100 + 4 * T2 * (i + 1)].rearrange("p (k n) -> p k n", k=4)
        XC, GT, RG, IG = (part(i) for i in range(4))
        ATL = flat_fa[:, 1100 + 16 * T2:1484 + 16 * T2]
        outb = QK[:].rearrange("p k n -> p (k n)")[:, 0:TT * D].rearrange("p (t d) -> p t d", t=TT)
        TAIL = T2 - 32
        t2 = {n: (s[v[0]] if v else ctx.enter_context(nc.semaphore(n))) for n, v in AGAIN.items()}
        t2["steps2"] = ctx.enter_context(nc.semaphore("steps2"))

        def at(name, n):
            old = AGAIN[name]
            return t2[name], (old[1] if old and name != "steps2" else 0) + n

        def layer_slab(l, i):
            if i < 10:
                a = [0, 256, 512, 768, 1024, 1280, 1536, 1792, 2048, 2304][i]
                return 8, 256, w_in_2[l, :, a:a + 256]
            if i < 14:
                return 8, 256, w_out_2[l, :, 256 * (i - 10):256 * (i - 10) + 256]
            if i < 36:
                a = 256 * ((i - 14) // 2) + FF * ((i - 14) % 2)
                return 8, 256, w_gu_2[l, :, a:a + 256]
            m, half = (i - 36) // 2, (i - 36) % 2
            return 11, P, w_down_2[l, 11 * P * half:11 * P * half + 11 * P, P * m:P * m + P]

        def sync_block2(sp):
            with sp.Fori(0, L2) as l:
                for i in range(LAYER_SLABS):
                    if i == 6:
                        sp.wait_ge(q1["acc_done"], 1)
                        sp.wait_ge(*at("gates_made", 4 * l))
                        for r, src in enumerate((w_rg_2, w_ig_2)):
                            for half in range(2):
                                sp.dma_start(WG[HD2 * half:HD2 * half + HD2, r, :, :],
                                             src[l].rearrange("(a two) d e -> two d a e", two=2)[half]).then_inc(t2["gate_w_in"], 16)
                    sp.wait_ge(s["slab_used"], USED_BLOCK2 + LAYER_SLABS * l + i - SLOTS + 1)
                    k, n, src = layer_slab(l, i)
                    sp.dma_start(slab(i % SLOTS, k, n), src.rearrange("(k p) n -> p k n", p=P)).then_inc(slot_in[i % SLOTS], 16)
            sp.wait_ge(*at("rows_out", 4))
            sp.dma_start(out[0].rearrange("(t p) d -> p t d", p=P), outb).then_inc(t2["stored"], 16)
            sp.wait_ge(t2["stored"], 16)

        def tensor_block2(pe):
            mm, tp, ident = pe.matmul, pe.transpose, C["ident"]

            def mean(dst, n):
                for k in range(n):
                    ins = mm(dst, ones[:], sq[:, k, 0:dst.shape[1]], start=(k == 0), stop=(k == n - 1))
                return ins

            pe.wait_ge(*at("m_sq", 1))
            mean(pb[0][:, 0:S], KD_).then_inc(t2["m_summed"], 1)

            with pe.Fori(0, L2) as l:
                def arrive(i):
                    slot, before = i % SLOTS, filled_before(i % SLOTS) + (E if i % SLOTS < EXPERT_SLABS else 0)
                    pe.wait_ge(slot_in[slot], 16 * (before + 4 * l + i // SLOTS + 1))
                    return slab(slot, 8, 256) if i < 36 else slab(slot, 11, P)

                def chunk(bank, w, m, src):
                    for k in range(KD_):
                        ins = mm(bank[:, 0:T2], w[:, k, P * m:P * m + P], src[:, k, :], start=(k == 0), stop=(k == KD_ - 1))
                    return ins

                pe.wait_ge(*at("n_sq", l + 1))
                mean(pb[0][:, 0:T2], KD_).then_inc(t2["n_summed"], 1)
                pe.wait_ge(*at("n_h", l + 1))

                def unit(u):
                    if u >= 4:
                        pe.wait_ge(*at("z2_out", 20 * l + u - 3))
                    return pb[u % 4]

                def units(i, u):
                    w = arrive(i)
                    for m in range(2):
                        ins = chunk(unit(u + m), w, m, hT)
                        if m == 0:
                            ins.then_inc(t2["z2_made"], 1)
                    ins.then_inc(s["slab_used"], 1)
                    mm(pb[7][:, 511:512], mean_d[:], ones[:, 0:1], start=True, stop=True).then_inc(t2["z2_made"], 1)

                for i in range(4):
                    units(i, 2 * i)
                for r in range(2):
                    pe.wait_ge(*at("qk_sq", 2 * l + r + 1))
                    if r == 1:
                        pe.wait_ge(*at("qk_root", 8 * l + 4))
                    for k in range(4):
                        ins = mm(pb[4 + k][:, 0:T2], C["halves"], sq[:, 4 * r + k, :], start=True, stop=True)
                        ins.then_inc(t2["qk_mean"], 1)
                for j in range(2):
                    w = arrive(4 + j)
                    bank = unit(8 + 2 * j)
                    for t in range(2):
                        for k in range(KD_):
                            ins = mm(bank[:, 256 * t:256 * t + 256], hT[:, k, P * t:P * t + P], w[:, k, :], start=(k == 0), stop=(k == KD_ - 1))
                    ins.then_inc(t2["z2_made"], 1)
                    bank = unit(9 + 2 * j)
                    for k in range(KD_):
                        ins = mm(bank[0:META, 0:256], hT[:, k, 2 * P:T2], w[:, k, :], start=(k == 0), stop=(k == KD_ - 1))
                    ins.then_inc(s["slab_used"], 1)
                    mm(bank[:, 511:512], mean_d[:], ones[:, 0:1], start=True, stop=True).then_inc(t2["z2_made"], 1)
                pe.wait_ge(*at("qk_root", 8 * l + 8))
                for r in range(2):
                    pe.wait_ge(*at("qk_normed", 2 * l + r + 1))
                    if r == 1:
                        pe.wait_ge(*at("rot_out", 8 * l + 4))
                    for k in range(4):
                        mm(pb[4 + k][:, 0:T2], C["rot"], QK[:, 4 * r + k, :], start=True, stop=True).then_inc(t2["qk_turned"], 1)
                for i in range(6, 10):
                    w = arrive(i)
                    u = 12 + 2 * (i - 6)
                    for m in range(2):
                        ins = chunk(unit(u + m), w, m, hT)
                        if m == 0:
                            ins.then_inc(t2["z2_made"], 1)
                    ins.then_inc(s["slab_used"], 1)
                    mm(pb[(u + 1) % 4][:, 511:512], mean_d[:], ones[:, 0:1], start=True, stop=True).then_inc(t2["z2_made"], 1)

                pe.wait_ge(*at("roped", 2 * l + 2))
                pe.wait_ge(*at("z2_out", 20 * l + 20))

                def scores(h):
                    if h >= 1:
                        pe.wait_ge(*at("prob2", 4 * l + h))
                    for c in range(2):
                        r = slice(HD2 * c, HD2 * c + HD2)
                        bank = pb[c]
                        mm(bank[:, 0:P], QK[r, h, 0:P], QK[r, 4 + h, 0:P], start=True, stop=False, skip_group_check=True)
                        mm(bank[:, 0:P], ident, C["future"], start=False, stop=False, skip_group_check=True)
                        mm(bank[:, P:384], QK[r, h, P:2 * P], QK[r, 4 + h, 0:2 * P], start=False, stop=False, skip_group_check=True)
                        ins = mm(bank[:, 256:384], ident, C["future"], start=False, stop=True, skip_group_check=True)
                    ins.then_inc(t2["scored2"], 1)

                def turn(h):
                    pe.wait_ge(*at("mixed2", 4 * l + h + 1))
                    if h >= 2:
                        pe.wait_ge(*at("at2", 4 * l + h - 1))
                    for b in range(3):
                        ins = tp(pb[2 + h % 2][:, P * b:P * b + P], PB[:, h % 2, 0, P * b:P * b + P], ident)
                    ins.then_inc(t2["turned2"], 1)

                def values(h):
                    pe.wait_ge(*at("at2", 4 * l + h + 1))
                    if h >= 2:
                        pe.wait_ge(*at("o2_out", 4 * l + h - 1))
                    bank, a, e = pb[4 + h % 2], AT[:, h % 2, :], slice(P * h, P * h + P)
                    own = 32 * h + 16
                    mm(bank[:, 0:256], V2[:, 0, e], a[:, 0:256], start=True, stop=False, skip_group_check=True)
                    mm(bank[:, P:256], V2[:, 1, e], a[:, 256:384], start=False, stop=False, skip_group_check=True)
                    mm(bank[:, 256:T2], V2[:, 0, e], ATL[:, own:own + 16], start=False, stop=False, skip_group_check=True)
                    mm(bank[:, 256:T2], V2[:, 1, e], ATL[:, P + own:P + own + 16], start=False, stop=False, skip_group_check=True)
                    mm(bank[:, 256:T2], V2[0:META, 2, e], ATL[0:META, 2 * P + own:2 * P + own + 16], start=False, stop=True,
                       skip_group_check=True).then_inc(t2["o2_made"], 1)

                scores(0)
                for c in range(2):
                    r = slice(HD2 * c, HD2 * c + HD2)
                    for h in range(H2):
                        mm(pb[6 + c][32 * h:32 * h + 32, 0:T2], QK[r, h, TAIL:T2], QK[r, 4 + h, :], start=True, stop=False,
                           skip_group_check=True)
                    mm(pb[6 + c][:, TAIL:T2], ident, C["future_tail"], start=False, stop=True, skip_group_check=True)\
                        .then_inc(t2["tail_scored"], 1)
                pe.wait_ge(*at("tail_mixed", l + 1))
                for b in range(3):
                    n = min(P, T2 - P * b)
                    ins = tp(pb[5][0:n, P * b:P * b + P], PL[:, 0, P * b:P * b + n], ident)
                ins.then_inc(t2["tail_turned"], 1)
                for c in range(4):
                    pe.wait_ge(*at("xc_ready", l + 1))
                    pe.wait_ge(t2["gate_w_in"], 64 * (l + 1))
                    if c >= 1:
                        pe.wait_ge(*at("gates_sig", 4 * l + c))
                    mm(pb[7][:, 511:512], mean_d[:], ones[:, 0:1], start=True, stop=True)
                    for r in range(2):
                        for half in range(2):
                            q = slice(HD2 * half, HD2 * half + HD2)
                            ins = mm(pb[6 + r][q, 0:T2], WG[q, r, c, :], XC[q, c, :], start=True, stop=True)
                    ins.then_inc(t2["gates_made"], 1)
                pe.wait_ge(*at("tail_t", l + 1))
                for h in range(H2):
                    turn(h)
                    if h + 1 < H2:
                        scores(h + 1)
                    values(h)
                pe.wait_ge(*at("o2_out", 4 * l + 4))
                for h in range(H2):
                    mm(pb[h][:, 0:T2], ones[:], sq[:, h, :], start=True, stop=True).then_inc(t2["o2_mean"], 1)
                pe.wait_ge(*at("rec_sq", l + 1))
                for k in range(4):
                    ins = mm(pb[6][:, 0:T2], ones[:], sq[:, 4 + k, :], start=(k == 0), stop=(k == 3))
                ins.then_inc(t2["rec_mean"], 1)
                pe.wait_ge(*at("mix_ready", l + 1))
                for i in range(10, 14):
                    w = arrive(i)
                    for m in range(2):
                        n = 2 * (i - 10) + m
                        if n >= 4:
                            pe.wait_ge(*at("out2_added", 8 * l + n - 3))
                        ins = chunk(pb[n % 4], w, m, yT)
                        if m == 0:
                            ins.then_inc(t2["out2_made"], 1)
                    ins.then_inc(s["slab_used"], 1)
                    mm(pb[7][:, 511:512], mean_d[:], ones[:, 0:1], start=True, stop=True).then_inc(t2["out2_made"], 1)
                pe.wait_ge(*at("f_sq", l + 1))
                mean(pb[4][:, 0:T2], KD_).then_inc(t2["f_summed"], 1)
                pe.wait_ge(*at("f_h", l + 1))
                for j in range(NF // 2):
                    if j >= 2:
                        pe.wait_ge(*at("gu_out", 11 * l + j - 1))
                    for r in range(2):
                        w = arrive(14 + 2 * j + r)
                        for m in range(2):
                            ins = chunk(pb[4 * (j % 2) + 2 * r + m], w, m, hT)
                        ins.then_inc(s["slab_used"], 1)
                    mm(pb[4 * (j % 2) + 3][:, 511:512], mean_d[:], ones[:, 0:1], start=True, stop=True).then_inc(t2["gu_made"], 1)
                pe.wait_ge(*at("gu_out", 11 * l + 11))
                for m in range(KD_):
                    if m >= 4:
                        pe.wait_ge(*at("down_added", 8 * l + m - 3))
                    for half in range(2):
                        w = arrive(36 + 2 * m + half)
                        for k in range(11):
                            kk = 11 * half + k
                            ins = mm(pb[m % 4][:, 0:T2], w[:, k, :], FA[:, kk, :], start=(kk == 0), stop=(kk == NF - 1))
                        ins.then_inc(s["slab_used"], 1)
                    mm(pb[m % 4][:, 511:512], mean_d[:], ones[:, 0:1], start=True, stop=True).then_inc(t2["down_made"], 1)

            pe.wait_ge(*at("down_added", 8 * L2))
            for b in range(4):
                for i in range(4):
                    k = 4 * (b % 2) + i
                    a = META + P * (b // 2)
                    ins = tp(pb[b][:, P * i:P * i + P], xT[:, k, a:a + P], ident)
                ins.then_inc(t2["x_out"], 1)

        def scalar_block2(act):
            def root(dst, src, scale):
                return act.activation(dst, src, ACT.Sqrt, bias=eps[:], scale=scale)

            for b in range(4):
                ins = act.activation(yv[:, 2 * b:2 * b + 2, :], pb[4 + b][:].rearrange("p (k n) -> p k n", k=2), ACT.Copy)
            ins.then_inc(t2["m_y"], 1)
            act.wait_ge(*at("m_summed", 1))
            root(rstd[:, 0:S], pb[0][:, 0:S], 1.0 / D).then_inc(t2["m_root"], 1)
            with act.Fori(0, L2) as l:
                act.wait_ge(*at("n_summed", l + 1))
                root(rstd[:], pb[0][:, 0:T2], 1.0 / D).then_inc(t2["n_root"], 1)
                for u in range(8):
                    act.wait_ge(*at("z2_made", 20 * l + u + 1))
                    act.activation(QK[:, u, :], pb[u % 4][:, 0:T2], ACT.Copy).then_inc(t2["z2_out"], 1)
                for k in range(8):
                    act.wait_ge(*at("qk_mean", 8 * l + k + 1))
                    root(sq[:, k, :], pb[4 + k % 4][:, 0:T2], 1.0).then_inc(t2["qk_root"], 1)
                for j in range(2):
                    act.wait_ge(*at("z2_made", 20 * l + 9 + 2 * j))
                    act.activation(V2[:, 0:2, 256 * j:256 * j + 256], pb[2 * j][:].rearrange("p (t n) -> p t n", t=2), ACT.Copy)\
                       .then_inc(t2["z2_out"], 1)
                    act.wait_ge(*at("z2_made", 20 * l + 10 + 2 * j))
                    act.activation(V2[0:META, 2, 256 * j:256 * j + 256], pb[1 + 2 * j][0:META, 0:256], ACT.Copy)\
                       .then_inc(t2["z2_out"], 1)
                for u in range(12, 20):
                    act.wait_ge(*at("z2_made", 20 * l + u + 1))
                    dst = XR[:, u - 12, 3:3 + T2] if u < 16 else GT[:, u - 16, :]
                    act.activation(dst, pb[u % 4][:, 0:T2], ACT.Copy).then_inc(t2["z2_out"], 1)
                act.wait_ge(*at("tail_max", l + 1))
                for c in range(2):
                    ins = act.activation(PL[:, c, :], pb[6 + c][:, 0:T2], ACT.Exp, bias=ST[:, 0, 0, c:c + 1], accum_out=ST[:, 0, 1, c:c + 1])
                ins.then_inc(t2["tail_prob"], 1)

                def exps(h):
                    act.wait_ge(*at("max2", 4 * l + h + 1))
                    if h >= 2:
                        act.wait_ge(*at("turned2", 4 * l + h - 1))
                    for c in range(2):
                        for t in range(2):
                            a, n = (0, P) if t == 0 else (P, 2 * P)
                            ins = act.activation(PB[:, h % 2, c, a:a + n], pb[c][:, a:a + n], ACT.Exp,
                                                 bias=ST2[:, h % 2, 0, 2 * c + t:2 * c + t + 1],
                                                 accum_out=ST2[:, h % 2, 1, 2 * c + t:2 * c + t + 1])
                    ins.then_inc(t2["prob2"], 1)

                exps(0)
                act.wait_ge(*at("tail_turned", l + 1))
                act.activation(ATL[:, 0:2 * P], pb[5][:, 0:2 * P], ACT.Copy)
                act.activation(ATL[0:META, 2 * P:384], pb[5][0:META, 2 * P:384], ACT.Copy).then_inc(t2["tail_t"], 1)
                for c in range(4):
                    act.wait_ge(*at("gates_made", 4 * l + c + 1))
                    act.activation(RG[:, c, :], pb[6][:, 0:T2], ACT.Sigmoid, bias=PC[:, bass.ds(r2["b_rg_2"] + 4 * l + c, 1)])
                    act.activation(IG[:, c, :], pb[7][:, 0:T2], ACT.Sigmoid, bias=PC[:, bass.ds(r2["b_ig_2"] + 4 * l + c, 1)])\
                       .then_inc(t2["gates_sig"], 1)
                for h in range(H2):
                    act.wait_ge(*at("turned2", 4 * l + h + 1))
                    if h >= 2:
                        act.wait_ge(*at("o2_made", 4 * l + h - 1))
                    act.activation(AT[:, h % 2, :], pb[2 + h % 2][:, 0:384], ACT.Copy).then_inc(t2["at2"], 1)
                    if h + 1 < H2:
                        exps(h + 1)
                    act.wait_ge(*at("o2_made", 4 * l + h + 1))
                    bank = pb[4 + h % 2][:, 0:T2]
                    act.activation(yT[:, h, :], bank, ACT.Copy)
                    act.activation(sq[:, h, :], bank, ACT.Square).then_inc(t2["o2_out"], 1)
                act.wait_ge(*at("gelu_in", l + 1))
                for c in range(4):
                    act.activation(FSv[:, c, :], RG[:, c, :], ACT.Tanh, scale=lru_c[:, 2, bass.ds(4 * l + c, 1)])
                for c in range(4):
                    ins = act.activation(RG[:, c, :], RG[:, c, :], ACT.Exp, scale=lru_c[:, 1, bass.ds(4 * l + c, 1)])
                ins.then_inc(t2["lru_exp"], 1)
                act.activation(hT[:, 0:4, :], hT[:, 0:4, :], ACT.Sigmoid, scale=2.0 * math.sqrt(2.0 / math.pi)).then_inc(t2["gelu_sig"], 1)
                act.wait_ge(*at("mult_in", l + 1))
                act.activation(FSv, FSv, ACT.Sqrt).then_inc(t2["mult_out"], 1)
                for h in range(H2):
                    act.wait_ge(*at("o2_mean", 4 * l + h + 1))
                    root(sq[:, h, :], pb[h][:, 0:T2], 1.0 / P).then_inc(t2["o2_root"], 1)
                act.wait_ge(*at("rec_mean", l + 1))
                root(rstd[:], pb[6][:, 0:T2], 1.0 / REC).then_inc(t2["rec_root"], 1)
                act.wait_ge(*at("f_summed", l + 1))
                root(rstd[:], pb[4][:, 0:T2], 1.0 / D).then_inc(t2["f_root"], 1)
                for j in range(NF // 2):
                    act.wait_ge(*at("gu_made", 11 * l + j + 1))
                    if j >= 2:
                        act.wait_ge(*at("gu_out", 11 * l + j - 1))
                    for m in range(2):
                        ins = act.activation(FS[:, 2 * (j % 2) + m, :], pb[4 * (j % 2) + m][:, 0:T2], ACT.Sigmoid)
                    ins.then_inc(t2["g_sig"], 1)
            for b in range(4):
                act.wait_ge(*at("x_out", b + 1))
                act.activation(outb[:, b // 2, 512 * (b % 2):512 * (b % 2) + 512], pb[b][:], ACT.Copy).then_inc(t2["rows_out"], 1)

        def vector_block2(dve):
            tt, ts, stt = dve.tensor_tensor, dve.tensor_scalar, dve.scalar_tensor_tensor
            st = Steps(dve, t2["steps2"])
            dve.wait_ge(*at("m_y", 1))
            tt(sqv, yv, yv, ALU.mult).then_inc(t2["m_sq"], 1)
            dve.wait_ge(*at("m_root", 1))
            st(dve.reciprocal(rstd[:, 0:S], rstd[:, 0:S]))
            st(tt(sqv, yv, spread(rstd[:, 0:S], KD_), ALU.mult))
            for k in range(KD_):
                ins = stt(xv[:, k, :], sqv[:, k, :], gt2[:, k:k + 1], xv[:, k, :], ALU.mult, ALU.add)
            st(ins)
            st(dve.memset(XR[:, :, 0:3], 0.0))
            first = st.n

            with dve.Fori(0, L2) as l:
                st = Steps(dve, t2["steps2"], first + VECTOR_STEPS * l)
                col = lambda name, k: PC[:, bass.ds(r2[name] + k, 1)]
                tt(sq[:], xT[:], xT[:], ALU.mult).then_inc(t2["n_sq"], 1)
                dve.wait_ge(*at("n_root", l + 1))
                st(dve.reciprocal(rstd[:], rstd[:]))
                for k in range(KD_):
                    ins = stt(hT[:, k, :], xT[:, k, :], col("norm_mix_g_2", 8 * l + k), rstd[:], ALU.mult, ALU.mult)
                ins.then_inc(t2["n_h"], 1)
                for r in range(2):
                    dve.wait_ge(*at("z2_out", 20 * l + 4 * r + 4))
                    half = QK[:, 4 * r:4 * r + 4, :]
                    tt(sq[:, 4 * r:4 * r + 4, :], half, half, ALU.mult).then_inc(t2["qk_sq"], 1)
                for r in range(2):
                    dve.wait_ge(*at("qk_root", 8 * l + 4 * r + 4))
                    half, part_ = QK[:, 4 * r:4 * r + 4, :], sq[:, 4 * r:4 * r + 4, :]
                    st(dve.reciprocal(part_, part_))
                    g = gains[:, 0, bass.ds(l, 1)] if r == 0 else col("k_norm_g_2", l)
                    stt(half, half, g, part_, ALU.mult, ALU.mult).then_inc(t2["qk_normed"], 1)
                for r in range(2):
                    half, part_ = QK[:, 4 * r:4 * r + 4, :], sq[:, 4 * r:4 * r + 4, :]
                    dve.wait_ge(*at("qk_normed", 2 * l + r + 1))
                    st(tt(part_, half, spread(C["cos"], 4), ALU.mult))
                    for k in range(4):
                        dve.wait_ge(*at("qk_turned", 8 * l + 4 * r + k + 1))
                        ins = tt(QK[:, 4 * r + k, :], pb[4 + k][:, 0:T2], C["sin"], ALU.mult)
                        ins.then_inc(t2["rot_out"], 1)
                    dve.wait_ge(*at("rot_out", 8 * l + 4 * r + 4))
                    tt(half, half, part_, ALU.add).then_inc(t2["roped"], 1)
                dve.wait_ge(*at("z2_out", 20 * l + 16))
                for w in (3, 2, 1, 0):
                    for c in range(4):
                        src = XR[:, c, w:w + T2]
                        cw = col("conv_w_2", 16 * l + 4 * w + c)
                        if w == 3:
                            ins = ts(XC[:, c, :], src, cw, col("conv_b_2", 4 * l + c), ALU.mult, ALU.add)
                        else:
                            ins = stt(XC[:, c, :], src, cw, XC[:, c, :], ALU.mult, ALU.add)
                    if w:
                        st(ins)
                ins.then_inc(t2["xc_ready"], 1)

                dve.wait_ge(*at("tail_scored", 2 * l + 2))
                for c in range(2):
                    ins = dve.tensor_reduce(ST[:, 0, 0, c:c + 1], pb[6 + c][:, 0:T2], AX_X, ALU.max, negate=True)
                ins.then_inc(t2["tail_max"], 1)
                minus = lam[:, bass.ds(l, 1)]

                def maxes(h):
                    dve.wait_ge(*at("scored2", 4 * l + h + 1))
                    for c in range(2):
                        for t in range(2):
                            a, n = (0, P) if t == 0 else (P, 2 * P)
                            ins = dve.tensor_reduce(ST2[:, h % 2, 0, 2 * c + t:2 * c + t + 1], pb[c][:, a:a + n], AX_X, ALU.max, negate=True)
                    ins.then_inc(t2["max2"], 1)

                def mix(h):
                    dve.wait_ge(*at("prob2", 4 * l + h + 1))
                    sums = ST2[:, h % 2, 1, :]
                    st(dve.reciprocal(sums, sums))
                    st(ts(sums[:, 2:4], sums[:, 2:4], minus, None, ALU.mult))
                    for t in range(2):
                        a = slice(0, P) if t == 0 else slice(P, 384)
                        ins = ts(PB[:, h % 2, 0, a], PB[:, h % 2, 0, a], sums[:, t:t + 1], None, ALU.mult)
                    st(ins)
                    for t in range(2):
                        a = slice(0, P) if t == 0 else slice(P, 384)
                        ins = stt(PB[:, h % 2, 0, a], PB[:, h % 2, 1, a], sums[:, 2 + t:3 + t], PB[:, h % 2, 0, a], ALU.mult, ALU.add)
                    ins.then_inc(t2["mixed2"], 1)

                maxes(0)
                dve.wait_ge(*at("tail_prob", l + 1))
                tail = ST[:, 0, 1, :]
                st(dve.reciprocal(tail[:, 0:2], tail[:, 0:2]))
                st(ts(tail[:, 1:2], tail[:, 1:2], minus, None, ALU.mult))
                st(ts(PL[:, 0, :], PL[:, 0, :], tail[:, 0:1], None, ALU.mult))
                stt(PL[:, 0, :], PL[:, 1, :], tail[:, 1:2], PL[:, 0, :], ALU.mult, ALU.add).then_inc(t2["tail_mixed"], 1)
                mix(0)
                g, inner = GT[:], hT[:, 0:4, :]
                dve.wait_ge(*at("z2_out", 20 * l + 20))
                st(tt(inner, g, g, ALU.mult))
                st(ts(inner, inner, 0.044715, 1.0, ALU.mult, ALU.add))
                dve.wait_ge(*at("gates_sig", 4 * l + 4))
                tt(inner, inner, g, ALU.mult).then_inc(t2["gelu_in"], 1)
                for h in range(1, H2):
                    maxes(h)
                    mix(h)
                dve.wait_ge(*at("lru_exp", l + 1))
                work = hT[:, 4:8, :]
                st(ts(work, FSv, 1.0, None, ALU.add))
                st(dve.reciprocal(work, work))
                stt(FSv, FSv, 2.0, work, ALU.mult, ALU.mult).then_inc(t2["mult_in"], 1)
                dve.wait_ge(*at("gelu_sig", l + 1))
                st(tt(GT[:], GT[:], inner, ALU.mult))
                st(tt(XC, XC, IG, ALU.mult))
                dve.wait_ge(*at("mult_out", l + 1))
                st(dve.memset(FSv[:, :, 0:1], 1.0))
                st(tt(XC, XC, FSv, ALU.mult))
                for c in range(4):
                    ins = dve.tensor_tensor_scan(IG[:, c, :], RG[:, c, :], XC[:, c, :], 0.0, ALU.mult, ALU.add)
                st(ins)
                st(tt(XC, IG, GT, ALU.mult))
                tt(sq[:, 4:8, :], XC, XC, ALU.mult).then_inc(t2["rec_sq"], 1)
                dve.wait_ge(*at("o2_root", 4 * l + 4))
                st(dve.reciprocal(sq[:, 0:4, :], sq[:, 0:4, :]))
                stt(yT[:, 0:4, :], yT[:, 0:4, :], gains[:, 1, bass.ds(l, 1)], sq[:, 0:4, :], ALU.mult, ALU.mult)
                dve.wait_ge(*at("rec_root", l + 1))
                st(dve.reciprocal(rstd[:], rstd[:]))
                for c in range(4):
                    ins = stt(yT[:, 4 + c, :], XC[:, c, :], col("rec_norm_g_2", 4 * l + c), rstd[:], ALU.mult, ALU.mult)
                ins.then_inc(t2["mix_ready"], 1)
                for m in range(KD_):
                    dve.wait_ge(*at("out2_made", 8 * l + m + 1))
                    tt(xT[:, m, :], pb[m % 4][:, 0:T2], xT[:, m, :], ALU.add).then_inc(t2["out2_added"], 1)
                dve.wait_ge(*at("out2_added", 8 * l + 8))
                tt(sq[:], xT[:], xT[:], ALU.mult).then_inc(t2["f_sq"], 1)
                dve.wait_ge(*at("f_root", l + 1))
                st(dve.reciprocal(rstd[:], rstd[:]))
                for k in range(KD_):
                    ins = stt(hT[:, k, :], xT[:, k, :], col("norm_ffn_g_2", 8 * l + k), rstd[:], ALU.mult, ALU.mult)
                ins.then_inc(t2["f_h"], 1)
                for j in range(NF // 2):
                    dve.wait_ge(*at("g_sig", 11 * l + j + 1))
                    for m in range(2):
                        gs = FS[:, 2 * (j % 2) + m, :]
                        ins = tt(gs, pb[4 * (j % 2) + m][:, 0:T2], gs, ALU.mult)
                    st(ins)
                    for m in range(2):
                        ins = tt(FA[:, 2 * j + m, :], pb[4 * (j % 2) + 2 + m][:, 0:T2], FS[:, 2 * (j % 2) + m, :], ALU.mult)
                    ins.then_inc(t2["gu_out"], 1)
                for m in range(KD_):
                    dve.wait_ge(*at("down_made", 8 * l + m + 1))
                    tt(xT[:, m, :], pb[m % 4][:, 0:T2], xT[:, m, :], ALU.add).then_inc(t2["down_added"], 1)
                dve.wait_ge(*at("down_added", 8 * l + 8))
                st(dve.memset(XR[:, :, 0:3], 0.0))
                assert st.n == VECTOR_STEPS, st.n

        block = ctx.enter_context(nc.Block())

        @block.sync
        def _(sp):
            sync_block1(sp)
            sync_experts(sp)
            sync_block2(sp)

        @block.gpsimd
        def _(pool):
            gpsimd_block1(pool)

        @block.scalar
        def _(act):
            scalar_loads(act)
            scalar_block1(act)
            scalar_experts(act)
            scalar_block2(act)

        @block.vector
        def _(dve):
            vector_block1(dve)
            vector_experts(dve)
            vector_block2(dve)

        @block.tensor
        def _(pe):
            tensor_block1(pe)
            tensor_experts(pe)
            tensor_block2(pe)


_INS = ['x', 'c', 'w_ada', 'b_ada', 'g_pre_mix', 'g_post_mix', 'g_pre_ffn', 'g_post_ffn', 'w_in', 'b_gates', 'conv_qk',
        'w_cmp_k', 'w_cmp_v', 'pos_cmp_k', 'pos_cmp_v', 'rel_bias', 'w_out', 'w_router', 'b_router', 'w_up', 'b_up',
        'w_down', 'b_down', 'meta_tokens_2', 'norm_mix_g_2', 'w_in_2', 'q_norm_g_2', 'k_norm_g_2', 'lambda_q1_2',
        'lambda_k1_2', 'lambda_q2_2', 'lambda_k2_2', 'subln_g_2', 'conv_w_2', 'conv_b_2', 'w_rg_2', 'b_rg_2',
        'w_ig_2', 'b_ig_2', 'lru_L_2', 'rec_norm_g_2', 'w_out_2', 'norm_ffn_g_2', 'w_gu_2', 'w_down_2']
_OUTS = [((1, S, D), 'float32')]


def kernel(**inputs):
    import numpy as _np
    import concourse.bacc as _bacc
    from concourse import mybir as _mybir
    from concourse.bass_utils import run_bass_kernel_spmd as _run

    nc = _bacc.Bacc("TRN2", target_bir_lowering=False, num_devices=1)
    arrays, args = {}, []
    for name in _INS + ['consts']:
        a = constants() if name == 'consts' else _np.ascontiguousarray(inputs[name])
        arrays[f"in_{name}_dram"] = a
        args.append(nc.dram_tensor(f"in_{name}_dram", a.shape, _mybir.dt.from_np(a.dtype), kind="ExternalInput").ap())
    for i, (shape, dtype) in enumerate(_OUTS):
        dt = _mybir.dt.from_np(_np.dtype(dtype))
        args.append(nc.dram_tensor(f"out_{i}_dram", shape, dt, kind="ExternalOutput").ap())
    build(nc, *args)
    r = _run(nc, [arrays], core_ids=[0])
    got = tuple(r.results[0][f"out_{i}_dram"] for i in range(len(_OUTS)))
    return got[0]
```
